# Optimizing a Trainium2 kernel written in Bass

```python
import math, functools
import jax, jax.numpy as jnp
from jax import lax
import numpy as np

D_MODEL = 1024
BATCH = 1
SEQ = 256
DEPTH = 2
DEC_BATCH = 1
DEC_SEQ = 32
PAST_LEN = 512

CHUNK = 64
N_EVEN = (DEPTH + 1) // 2
N_ODD = DEPTH // 2
EPS = 1e-6
CONV_W = 4
A_HEADS = 4
A_DK = 128
A_DV = 128
A_WIDTH = A_HEADS * A_DV
B_WIDTH = 512
B_BLOCKS = 8
B_BLOCK = B_WIDTH // B_BLOCKS
RG_C = 8.0
AB_IN = 4 * A_WIDTH + 2 * A_HEADS + 2 * B_WIDTH
AB_SPLITS = [3 * A_WIDTH, 4 * A_WIDTH, 4 * A_WIDTH + A_HEADS, 4 * A_WIDTH + 2 * A_HEADS,
             4 * A_WIDTH + 2 * A_HEADS + B_WIDTH]
C_HEADS = 8
C_DH = 64
C_VD = 2 * C_DH
C_WIDTH = C_HEADS * C_VD
Q_BLOCK = 128
PEER_HEADS = 8
N_KEYS = 128
N_EXPERTS = N_KEYS * N_KEYS
PEER_TOPK = 16
PEER_DQ = 256
PEER_BLOCK = 256

kernel_name = 'hybrid_gdn_rglru_diffattn_peer_stream_step'

def rmsnorm(x, g):
    x32 = x.astype(jnp.float32)
    y = x32 * lax.rsqrt(jnp.mean(x32 * x32, axis=-1, keepdims=True) + EPS)
    return (y * g.astype(jnp.float32)).astype(x.dtype)

def l2norm(x):
    x32 = x.astype(jnp.float32)
    return x32 * lax.rsqrt(jnp.sum(x32 * x32, axis=-1, keepdims=True) + EPS)

def causal_conv(x, prev, w):
    t = x.shape[1]
    xp = jnp.concatenate([prev.astype(x.dtype), x], axis=1)
    out = sum(xp[:, j:j + t] * w[j] for j in range(CONV_W))
    return out, xp[:, -(CONV_W - 1):]

def gated_delta_rule(q, k, v, g, beta, s0, chunk):
    f32 = jnp.float32
    bsz, t, nh, _ = q.shape
    dv = v.shape[-1]
    n = t // chunk

    def to_chunks(a):
        a = a.astype(f32).reshape((bsz, n, chunk, nh) + a.shape[3:])
        return jnp.moveaxis(a, (1, 3), (0, 2))

    q, k, v, g, beta = (to_chunks(a) for a in (q, k, v, g, beta))
    gc = jnp.cumsum(g, axis=-1)
    pos = jnp.arange(chunk)
    lower = pos[:, None] >= pos[None, :]
    decay = jnp.exp(jnp.where(lower, gc[..., :, None] - gc[..., None, :], -jnp.inf))
    kb = k * beta[..., None]
    a_strict = jnp.where(pos[:, None] > pos[None, :],
                         jnp.einsum('nbhid,nbhjd->nbhij', kb, k) * decay, 0.0)
    lhs = a_strict + jnp.eye(chunk, dtype=f32)
    solve = functools.partial(lax.linalg.triangular_solve, left_side=True, lower=True)
    u = solve(lhs, v * beta[..., None])
    w = solve(lhs, kb * jnp.exp(gc)[..., None])
    qk = jnp.einsum('nbhid,nbhjd->nbhij', q, k) * decay

    def step(s, xs):
        q_c, k_c, u_c, w_c, gc_c, qk_c = xs
        v_new = u_c - jnp.einsum('bhck,bhkv->bhcv', w_c, s)
        o_c = (jnp.einsum('bhck,bhkv->bhcv', q_c * jnp.exp(gc_c)[..., None], s)
               + jnp.einsum('bhij,bhjv->bhiv', qk_c, v_new))
        g_last = gc_c[..., -1:]
        s = (s * jnp.exp(g_last)[..., None]
             + jnp.einsum('bhck,bhcv->bhkv', k_c * jnp.exp(g_last - gc_c)[..., None], v_new))
        return s, o_c

    s_fin, o = lax.scan(step, s0.astype(f32), (q, k, u, w, gc, qk))
    o = jnp.moveaxis(o, (0, 2), (1, 3)).reshape(bsz, t, nh, dv)
    return o, s_fin

def lru_combine(c1, c2):
    a1, b1 = c1
    a2, b2 = c2
    return a1 * a2, a2 * b1 + b2

def mixer_ab(h, conv_a_prev, s0, conv_b_prev, h0, w_in, w_out, a_conv_w, a_log, a_dt_bias,
             a_norm, b_conv_w, b_conv_b, b_ga_w, b_ga_b, b_gx_w, b_gx_b, b_lambda, chunk):
    f32 = jnp.float32
    bsz, t, _ = h.shape
    qkv, z, beta_l, alpha_l, xb, gb = jnp.split(h @ w_in, AB_SPLITS, axis=-1)
    qkv, conv_a_new = causal_conv(qkv, conv_a_prev, a_conv_w)
    q, k, v = jnp.split(jax.nn.silu(qkv), 3, axis=-1)
    q = l2norm(q.reshape(bsz, t, A_HEADS, A_DK)) * A_DK ** -0.5
    k = l2norm(k.reshape(bsz, t, A_HEADS, A_DK))
    v = v.reshape(bsz, t, A_HEADS, A_DV)
    beta = jax.nn.sigmoid(beta_l.astype(f32))
    g = -jnp.exp(a_log.astype(f32)) * jax.nn.softplus(alpha_l.astype(f32) + a_dt_bias.astype(f32))
    o, s_new = gated_delta_rule(q, k, v, g, beta, s0, chunk)
    o = rmsnorm(o, a_norm).astype(h.dtype) * jax.nn.silu(z.reshape(bsz, t, A_HEADS, A_DV))
    xc, conv_b_new = causal_conv(xb, conv_b_prev, b_conv_w)
    xc = xc + b_conv_b
    xblk = xc.reshape(bsz, t, B_BLOCKS, B_BLOCK)
    r = jax.nn.sigmoid(jnp.einsum('btni,nij->btnj', xblk, b_ga_w).reshape(bsz, t, B_WIDTH) + b_ga_b)
    i = jax.nn.sigmoid(jnp.einsum('btni,nij->btnj', xblk, b_gx_w).reshape(bsz, t, B_WIDTH) + b_gx_b)
    log_a = -RG_C * r.astype(f32) * jax.nn.softplus(-b_lambda.astype(f32))
    a = jnp.exp(log_a)
    u = jnp.sqrt(-jnp.expm1(2.0 * log_a)) * (i * xc).astype(f32)
    u = u.at[:, 0].add(a[:, 0] * h0.astype(f32))
    _, hs = lax.associative_scan(lru_combine, (a, u), axis=1)
    ob = hs.astype(h.dtype) * jax.nn.gelu(gb)
    out = jnp.concatenate([o.reshape(bsz, t, A_WIDTH), ob], axis=-1) @ w_out
    return out, conv_a_new, s_new.astype(h.dtype), conv_b_new, hs[:, -1].astype(h.dtype)

def diff_attn_block(q, k, v, q_pos, k_pos, lam, lam_init, norm_g):
    s = jnp.einsum('bqhcd,bkhcd->bhcqk', q.astype(jnp.float32), k.astype(jnp.float32)) * C_DH ** -0.5
    mask = (k_pos[None, :] // CHUNK) <= (q_pos[:, None] // CHUNK)
    p = jax.nn.softmax(jnp.where(mask, s, -jnp.inf), axis=-1)
    p = p[:, :, 0] - lam * p[:, :, 1]
    o = jnp.einsum('bhqk,bkhe->bqhe', p, v.astype(jnp.float32))
    return rmsnorm(o, norm_g) * (1.0 - lam_init)

def mixer_c(h, k_past, v_past, q_pos, k_pos, w_qkv, w_out, lq1, lk1, lq2, lk2, norm_g, lam_init):
    f32 = jnp.float32
    bsz, t, _ = h.shape
    q, k, v = jnp.split(h @ w_qkv, 3, axis=-1)
    q = q.reshape(bsz, t, C_HEADS, 2, C_DH)
    k = k.reshape(bsz, t, C_HEADS, 2, C_DH)
    v = v.reshape(bsz, t, C_HEADS, C_VD)
    lam = (jnp.exp(jnp.sum(lq1.astype(f32) * lk1.astype(f32)))
           - jnp.exp(jnp.sum(lq2.astype(f32) * lk2.astype(f32))) + lam_init)
    if k_past is None:
        outs = []
        for qs in range(0, t, Q_BLOCK):
            qe = min(qs + Q_BLOCK, t)
            outs.append(diff_attn_block(q[:, qs:qe], k[:, :qe], v[:, :qe], q_pos[qs:qe], k_pos[:qe],
                                        lam, lam_init, norm_g))
        o = jnp.concatenate(outs, axis=1)
    else:
        k_all = jnp.concatenate([k_past.astype(h.dtype), k], axis=1)
        v_all = jnp.concatenate([v_past.astype(h.dtype), v], axis=1)
        o = diff_attn_block(q, k_all, v_all, q_pos, k_pos, lam, lam_init, norm_g)
    out = o.reshape(bsz, t, C_WIDTH).astype(h.dtype) @ w_out
    return out, k, v

def peer(h, w_query, sub_keys, u_emb, v_emb):
    f32 = jnp.float32
    bsz, t, d = h.shape
    n_tok = bsz * t
    pad = (-n_tok) % PEER_BLOCK
    hb = jnp.pad(h.reshape(n_tok, d), ((0, pad), (0, 0))).reshape(-1, PEER_BLOCK, d)

    def block(xb):
        qry = (xb @ w_query).astype(f32).reshape(PEER_BLOCK, PEER_HEADS, 2, PEER_DQ // 2)
        sc = jnp.einsum('thpd,pnd->thpn', qry, sub_keys.astype(f32))
        s1, i1 = lax.top_k(sc[:, :, 0], PEER_TOPK)
        s2, i2 = lax.top_k(sc[:, :, 1], PEER_TOPK)
        cand_s = (s1[..., :, None] + s2[..., None, :]).reshape(PEER_BLOCK, PEER_HEADS, PEER_TOPK * PEER_TOPK)
        cand_i = (i1[..., :, None] * N_KEYS + i2[..., None, :]).reshape(PEER_BLOCK, PEER_HEADS, PEER_TOPK * PEER_TOPK)
        top_s, sel = lax.top_k(cand_s, PEER_TOPK)
        idx = jnp.take_along_axis(cand_i, sel, axis=-1)
        gate = jax.nn.softmax(top_s, axis=-1)
        act = jax.nn.gelu(jnp.einsum('thed,td->the', u_emb[idx], xb).astype(f32))
        return jnp.einsum('the,thed->td', (gate * act).astype(xb.dtype), v_emb[idx])

    return lax.map(block, hb).reshape(-1, d)[:n_tok].reshape(bsz, t, d)

def trunk(x, st_a_conv, st_a_delta, st_b_conv, st_b_h, c_k, c_v, p, past):
    t = x.shape[1]
    chunk = min(CHUNK, t)
    q_pos = past + jnp.arange(t)
    k_pos = jnp.arange(past + t)
    a_conv, a_delta, b_conv, b_h, new_k, new_v = [], [], [], [], [], []
    for l in range(DEPTH):
        j = l // 2
        h = rmsnorm(x, p['norm_mix'][l])
        if l % 2 == 0:
            out, ca, sd, cb, hb = mixer_ab(
                h, st_a_conv[j], st_a_delta[j], st_b_conv[j], st_b_h[j],
                p['ab_w_in'][j], p['ab_w_out'][j], p['a_conv_w'][j], p['a_log'][j], p['a_dt_bias'][j],
                p['a_norm'][j], p['b_conv_w'][j], p['b_conv_b'][j], p['b_gate_a_w'][j], p['b_gate_a_b'][j],
                p['b_gate_x_w'][j], p['b_gate_x_b'][j], p['b_lambda'][j], chunk)
            a_conv.append(ca)
            a_delta.append(sd)
            b_conv.append(cb)
            b_h.append(hb)
        else:
            lam_init = 0.8 - 0.6 * math.exp(-0.3 * l)
            out, kn, vn = mixer_c(
                h, None if c_k is None else c_k[j], None if c_v is None else c_v[j], q_pos, k_pos,
                p['c_w_qkv'][j], p['c_w_out'][j], p['c_lambda_q1'][j], p['c_lambda_k1'][j],
                p['c_lambda_q2'][j], p['c_lambda_k2'][j], p['c_norm'][j], lam_init)
            new_k.append(kn)
            new_v.append(vn)
        x = x + out
        x = x + peer(rmsnorm(x, p['norm_ffn'][l]), p['peer_w_query'][l], p['peer_sub_keys'][l],
                     p['peer_u'][l], p['peer_v'][l])
    y = rmsnorm(x, p['norm_final'])
    return (y, jnp.stack(a_conv), jnp.stack(a_delta), jnp.stack(b_conv), jnp.stack(b_h),
            jnp.stack(new_k), jnp.stack(new_v))

def setup_inputs(seed: int = 0) -> dict:
    key = jax.random.key(seed)
    ks = jax.random.split(key, 40)
    f32 = jnp.float32
    d = D_MODEL

    def nrm(i, shape, scale):
        return jax.random.normal(ks[i], shape, f32) * scale

    def gain(i, shape):
        return 1.0 + 0.02 * jax.random.normal(ks[i], shape, f32)

    a_log = jnp.log(jax.random.uniform(ks[9], (N_EVEN, A_HEADS), f32, 1.0, 16.0))
    dt = jnp.exp(jax.random.uniform(ks[10], (N_EVEN, A_HEADS), f32, math.log(1e-3), math.log(1e-1)))
    a_dt_bias = dt + jnp.log(-jnp.expm1(-dt))
    ar = jax.random.uniform(ks[18], (N_EVEN, B_WIDTH), f32, 0.9, 0.999) ** (1.0 / RG_C)
    b_lambda = jnp.log(ar) - jnp.log1p(-ar)
    return {
        'x_prompt': nrm(0, (BATCH, SEQ, d), 1.0),
        'x_sample': nrm(1, (DEC_BATCH, DEC_SEQ, d), 1.0),
        'state_a_conv': nrm(2, (N_EVEN, DEC_BATCH, CONV_W - 1, 3 * A_WIDTH), 1.0),
        'state_a_delta': nrm(3, (N_EVEN, DEC_BATCH, A_HEADS, A_DK, A_DV), 0.1),
        'state_b_conv': nrm(4, (N_EVEN, DEC_BATCH, CONV_W - 1, B_WIDTH), 1.0),
        'state_b_rglru': nrm(5, (N_EVEN, DEC_BATCH, B_WIDTH), 0.5),
        'cache_c_k': nrm(6, (N_ODD, DEC_BATCH, PAST_LEN, C_HEADS, 2, C_DH), 1.0),
        'cache_c_v': nrm(7, (N_ODD, DEC_BATCH, PAST_LEN, C_HEADS, C_VD), 1.0),
        'norm_mix': gain(8, (DEPTH, d)),
        'norm_ffn': gain(11, (DEPTH, d)),
        'norm_final': gain(12, (d,)),
        'ab_w_in': nrm(13, (N_EVEN, d, AB_IN), d ** -0.5),
        'ab_w_out': nrm(14, (N_EVEN, A_WIDTH + B_WIDTH, d), (A_WIDTH + B_WIDTH) ** -0.5),
        'a_conv_w': nrm(15, (N_EVEN, CONV_W, 3 * A_WIDTH), CONV_W ** -0.5),
        'a_log': a_log,
        'a_dt_bias': a_dt_bias,
        'a_norm': gain(16, (N_EVEN, A_DV)),
        'b_conv_w': nrm(17, (N_EVEN, CONV_W, B_WIDTH), CONV_W ** -0.5),
        'b_conv_b': nrm(19, (N_EVEN, B_WIDTH), 0.02),
        'b_gate_a_w': nrm(20, (N_EVEN, B_BLOCKS, B_BLOCK, B_BLOCK), B_BLOCK ** -0.5),
        'b_gate_a_b': nrm(21, (N_EVEN, B_WIDTH), 0.02),
        'b_gate_x_w': nrm(22, (N_EVEN, B_BLOCKS, B_BLOCK, B_BLOCK), B_BLOCK ** -0.5),
        'b_gate_x_b': nrm(23, (N_EVEN, B_WIDTH), 0.02),
        'b_lambda': b_lambda,
        'c_w_qkv': nrm(24, (N_ODD, d, 3 * C_WIDTH), d ** -0.5),
        'c_w_out': nrm(25, (N_ODD, C_WIDTH, d), C_WIDTH ** -0.5),
        'c_lambda_q1': nrm(26, (N_ODD, C_DH), 0.1),
        'c_lambda_k1': nrm(27, (N_ODD, C_DH), 0.1),
        'c_lambda_q2': nrm(28, (N_ODD, C_DH), 0.1),
        'c_lambda_k2': nrm(29, (N_ODD, C_DH), 0.1),
        'c_norm': gain(30, (N_ODD, C_VD)),
        'peer_w_query': nrm(31, (DEPTH, d, PEER_HEADS * PEER_DQ), d ** -0.5),
        'peer_sub_keys': nrm(32, (DEPTH, 2, N_KEYS, PEER_DQ // 2), (PEER_DQ // 2) ** -0.5),
        'peer_u': nrm(33, (DEPTH, N_EXPERTS, d), d ** -0.5),
        'peer_v': nrm(34, (DEPTH, N_EXPERTS, d), PEER_HEADS ** -0.5),
    }

def reference(x_prompt, x_sample, state_a_conv, state_a_delta, state_b_conv, state_b_rglru,
              cache_c_k, cache_c_v, norm_mix, norm_ffn, norm_final, ab_w_in, ab_w_out, a_conv_w,
              a_log, a_dt_bias, a_norm, b_conv_w, b_conv_b, b_gate_a_w, b_gate_a_b, b_gate_x_w,
              b_gate_x_b, b_lambda, c_w_qkv, c_w_out, c_lambda_q1, c_lambda_k1, c_lambda_q2,
              c_lambda_k2, c_norm, peer_w_query, peer_sub_keys, peer_u, peer_v):
    p = dict(norm_mix=norm_mix, norm_ffn=norm_ffn, norm_final=norm_final, ab_w_in=ab_w_in,
             ab_w_out=ab_w_out, a_conv_w=a_conv_w, a_log=a_log, a_dt_bias=a_dt_bias, a_norm=a_norm,
             b_conv_w=b_conv_w, b_conv_b=b_conv_b, b_gate_a_w=b_gate_a_w, b_gate_a_b=b_gate_a_b,
             b_gate_x_w=b_gate_x_w, b_gate_x_b=b_gate_x_b, b_lambda=b_lambda, c_w_qkv=c_w_qkv,
             c_w_out=c_w_out, c_lambda_q1=c_lambda_q1, c_lambda_k1=c_lambda_k1,
             c_lambda_q2=c_lambda_q2, c_lambda_k2=c_lambda_k2, c_norm=c_norm,
             peer_w_query=peer_w_query, peer_sub_keys=peer_sub_keys, peer_u=peer_u, peer_v=peer_v)
    bp = x_prompt.shape[0]
    dt = x_prompt.dtype
    z_a_conv = jnp.zeros((N_EVEN, bp, CONV_W - 1, 3 * A_WIDTH), dt)
    z_a_delta = jnp.zeros((N_EVEN, bp, A_HEADS, A_DK, A_DV), dt)
    z_b_conv = jnp.zeros((N_EVEN, bp, CONV_W - 1, B_WIDTH), dt)
    z_b_h = jnp.zeros((N_EVEN, bp, B_WIDTH), dt)
    (y_prompt, pa_conv, pa_delta, pb_conv, pb_h, pc_k, pc_v) = trunk(
        x_prompt, z_a_conv, z_a_delta, z_b_conv, z_b_h, None, None, p, 0)
    (y_sample, sa_conv, sa_delta, sb_conv, sb_h, sc_k, sc_v) = trunk(
        x_sample, state_a_conv, state_a_delta, state_b_conv, state_b_rglru, cache_c_k, cache_c_v,
        p, cache_c_k.shape[2])
    return (y_prompt, y_sample, pa_conv, pa_delta, pb_conv, pb_h, pc_k, pc_v,
            sa_conv, sa_delta, sb_conv, sb_h, sc_k, sc_v)


_drawn_inputs = setup_inputs


def setup_inputs(seed=0):
    import zlib

    import numpy as np

    out = dict(_drawn_inputs(seed))
    spreads = {}
    factors = {'norm_final': 8.328, 'b_gate_a_b': 11.561, 'b_gate_x_b': 3.495, 'c_norm': 8.74}
    for name, (base, spread) in spreads.items():
        noise = np.random.default_rng([zlib.crc32(name.encode()), seed]).standard_normal(out[name].shape)
        drawn = base * np.exp(spread * noise) if base else spread * noise
        out[name] = __import__('jax').numpy.asarray(drawn.astype(out[name].dtype))
    for name, factor in factors.items():
        out[name] = (out[name] * factor).astype(out[name].dtype)
    return out
```

```python
import math
from contextlib import ExitStack

D = 1024
KT = D // 128
NP = 256
NS = 32
NT = NP + NS
H = 4
HC = 8
PAST = 512
EPS = 1e-6
TOPK = 16
NKEY = 128
PH = 8
WSLOTS = 4
UVS = 8
NEG = -1e30
B_IN, B_OUT0, B_Q0 = 0, 24, 32
B_QKV, B_OUT1, B_Q1 = 48, 72, 80
NBLK = 96
ARENA = 30700
C_CW, C_CB, C_AL, C_DT, C_LM, C_GA, C_GX, C_AN, C_CN, C_H0, NCOL = 0, 64, 68, 77, 86, 90, 94, 98, 99, 100, 104
TILES = {0: (0, 1, 2), 1: (0, 1, 2), 2: (2, 0, 1), 3: (0, 1, 2), 4: (2, 0, 1)}
LAM_INIT = 0.8 - 0.6 * math.exp(-0.3)


def build(nc, T, DEBUG=False):
    import concourse.bass as bass
    from concourse import mybir

    F, U = mybir.dt.float32, mybir.dt.uint32
    ALU, ACT, AX = mybir.AluOpType, mybir.ActivationFunctionType, mybir.AxisListType

    with ExitStack() as ctx:
        def sb(name, shape, dt=F):
            return ctx.enter_context(nc.sbuf_tensor("sb_" + name, shape, dt))

        sems = {}

        def S(name):
            if name not in sems:
                sems[name] = ctx.enter_context(nc.semaphore(name))
            return sems[name]

        class Chain:

            def __init__(self, eng, name):
                self.eng, self.name = eng, name
                self.sem, self.n, self.looping = S(name), 0, False

            def add(self, ins):
                self.n += 1
                ins.then_inc(self.sem, 1)

            def settle(self):
                if self.looping and self.n == 0:
                    return
                self.eng.wait_ge(self.sem, self.n)
                if self.looping:
                    self.eng.sem_clear(self.sem)
                    self.n = 0

            def link(self, ins):
                self.add(ins)
                self.settle()

            def loop(self):
                self.settle()
                self.kept, self.sem, self.n, self.looping = self.n, S(self.name + "_loop"), 0, True

            def loop_end(self):
                assert self.n == 0
                self.sem, self.n, self.looping = S(self.name), self.kept, False

        X = sb("X", [128, 3, D])
        Hn = sb("Hn", [128, 3, D])
        hT = sb("hT", [128, KT, 384])
        W = sb("W", [128, WSLOTS, KT * 128])
        gB = sb("gB", [128, D])
        cols = sb("cols", [128, NCOL])
        keysT = sb("keysT", [128, 2, 2, NKEY])
        ident = sb("ident", [128, 128])
        ones = sb("ones", [128, 128])
        bm16 = sb("bm16", [128, 128])
        bm32 = sb("bm32", [128, 128])
        bm64 = sb("bm64", [128, 128])
        mhalf = sb("mhalf", [128, 18])
        ss = sb("ss", [128, 18])
        rstd = sb("rstd", [128, 18])
        mixT = sb("mixT", [128, 8, 384])
        AR = sb("AR", [128, ARENA])
        PS = ctx.enter_context(nc.psum_tensor("PS", [128, 8, 512], F))

        class Arena:
            def __init__(self, at=0):
                self.at = at

            def __call__(self, *shape, dt=F):
                n = 1
                for s in shape:
                    n *= s
                v = AR[:, self.at:self.at + n]
                self.at += n
                assert self.at <= ARENA, self.at
                if dt is not F:
                    v = v.bitcast(dt)
                if len(shape) == 2:
                    return v.rearrange("p (a b) -> p a b", b=shape[1])
                if len(shape) == 3:
                    return v.rearrange("p (a b c) -> p a b c", b=shape[1], c=shape[2])
                return v

        a = Arena()
        PJ = a(16, 294)
        CV = a(16, 291)
        QK = a(8, 291)
        RN = a(8, 291)
        QU, KU, VU = a(9, 128), a(9, 128), a(9, 128)
        Dm, DT, E = a(9, 128), a(9, 128), a(9, 128)
        KBE, KDEC, BV = a(9, 128), a(9, 128), a(9, 128)
        SZ = a(4, NT)
        GG = a(4, NT)
        S0, S1, S2 = a(4, 128), a(4, 128), a(4, 128)
        GW = a(2, 4, 128)
        sm = a(256)
        MDT, MDTs, MDs, MDss = a(128), a(128), a(128), a(128)
        LTp, LTs = a(128), a(128)
        CSi = a(16, 3)
        CSo = a(16, 6)
        WBA = a(8, 8)
        mix0_end = a.at
        b = Arena(0)
        Am, AT_, P1, P1T = (b(9, 128) for _ in range(4))
        MX = mixT[:, :, :].rearrange("p a b -> p (a b)")
        TTm = MX[:, 0:1152].rearrange("p (a b) -> p a b", b=128)
        Tm = MX[:, 1536:2688].rearrange("p (a b) -> p a b", b=128)
        b = Arena(16 * 294)
        B1T, B2T, B3T = (b(9, 128) for _ in range(3))
        b = Arena(16 * 294 + 16 * 291)
        TD, TS, XM, NW = (b(9, 128) for _ in range(4))
        P2, P2T, P4, P4T, P8T = TD, TS, P1, P1T, TD
        VN = Dm
        VNm = TS[:, 0:4, :]
        ON = Am
        LR = Hn[:, :, :].rearrange("p a b -> p (a b)")
        L1 = LR[:, 0:4 * 291].rearrange("p (a b) -> p a b", b=291)
        L2 = LR[:, 4 * 291:8 * 291].rearrange("p (a b) -> p a b", b=291)
        HTf = hT[:, :, :].rearrange("p a b -> p (a b)")
        L3 = HTf[:, 0:4 * 291].rearrange("p (a b) -> p a b", b=291)
        L4 = HTf[:, 4 * 291:8 * 291].rearrange("p (a b) -> p a b", b=291)

        a = Arena()
        QZ = a(8 * 2, NT)
        KTt = a(8, NT)
        Vt = a(3, D)
        KC = a(8, PAST)
        VC = a(4, D)
        PP = a(2, 2 * 384)
        PC = a(2, 384)
        PTt = a(2, 384)
        OS = a(18, 128)
        lq = a(4, 64)
        la_ = a(64)
        msk = a(384)
        assert a.at <= ARENA
        b = Arena(16 * NT + 8 * NT + 3 * D + 8 * PAST + 4 * D)
        PPs = b(2, 544)
        b2 = Arena(b.at)
        PCs = b2(1, 544)

        a = Arena()
        UV = a(UVS, 2 * D)
        SC = a(2 * 16, NKEY)
        SCS = a(4, NKEY)
        QT = a(4, NT)
        assert a.at <= ARENA
        YS = QT.rearrange("p a b -> p (a b)")[:, 0:D]
        p = Arena(UVS * 2 * D + 36 * NKEY + 4 * NT)
        rows = p(2, NKEY)
        tm = p(2, NKEY)
        cand = p(16, 16)
        candt = p(16 * 16)
        hot = p(32, 16)
        pv_, pi = p(2, 16), p(2, 16, dt=U)
        tv, sel = p(16), p(16, dt=U)
        ab = p(32, dt=U)
        i12 = p(32)
        gsum = p(8)
        idx = sb("idx", [128, 288], U)
        idst = sb("idst", [128, 16], U)
        gate = sb("gate", [128, 288])
        iota16 = sb("iota16", [128, 16])
        dots = sb("dots", [128, 8])
        gl = sb("gl", [128, 8])
        gst = sb("gst", [128, 16])
        DG = sb("DG", [128, UVS, 128])
        ZR = sb("ZR", [128, 512])
        RP = sb("RP", [128, 128])
        BA = sm[:, 0:24]
        AL, TH, MN, EX, SR, SQ_, PL, SP = (sm[:, 24 + 13 * i:24 + 13 * (i + 1)] for i in range(8))
        BE, GC, NGC, EGC, BEG, DEC, EAL, G9 = (sm[:, 130 + 9 * i:139 + 9 * i] for i in range(8))
        EGL = sm[:, 204:213]
        CLM = sm[:, 214:218]
        HB = sm[:, 218:226]
        egls = sm[:, 226:230]
        hlast = sm[:, 232:240]

        def blkw(s, k):
            return W[:, s, 128 * k:128 * k + 128]

        def unit(v, u):
            return v[:, u, :]

        BT = [(0, 4), (4, 8), (8, 9)]
        INV = ["a2", "n2", "n4", "n8", "x1", "m1", "x2", "m2", "x3", "m3"]
        INV_A = {"a2": 1, "n2": 1, "n4": 1, "n8": 0, "x1": 1, "m1": 0, "x2": 1, "m2": 0, "x3": 1, "m3": 0}
        INV_V = {"a2": 1, "n2": 1, "n4": 1, "n8": 1, "x1": 0, "m1": 1, "x2": 0, "m2": 1, "x3": 0, "m3": 1}

        def inv_count(has, st, bt):
            n = 0
            for i, name in enumerate(INV):
                for t in range(3):
                    n += has[name]
                    if i == st and t == bt:
                        return n

        block = ctx.enter_context(nc.Block())

        @block.sync
        def _(eng):
            d = nc.sync.dma_start
            for t in range(3):
                d(X[:, t, :], T["x"][:, t, :]).then_inc(S(f"x_in{t}"), 16)
            d(gB[:, :], T["gains"][0:1, :].to_broadcast([128, D])).then_inc(S("gain"), 16)
            for s in range(WSLOTS):
                d(W[:, s, :], T["w"][s]).then_inc(S(f"w_in{s}"), 16)

            def stream(b0, b1):
                with eng.Fori(0, (b1 - b0) // WSLOTS) as i:
                    for s in range(WSLOTS):
                        eng.wait_ge(S("blk"), i * WSLOTS + (b0 + s + 1 - WSLOTS))
                        d(W[:, s, :], T["w"][bass.ds(i * WSLOTS + (b0 + s), 1), :, :]
                          .rearrange("a p n -> (a p) n")).then_inc(S(f"w_in{s}"), 16)

            stream(WSLOTS, B_OUT0)
            eng.wait_ge(S("cso"), 2)
            d(T["o_conv"], CSo.rearrange("p a b -> p (a b)")).then_inc(S("out"), 16)
            stream(B_OUT0, B_Q0 + WSLOTS)
            eng.wait_ge(S("Hn"), 3)
            d(gB[:, :], T["gains"][1:2, :].to_broadcast([128, D])).then_inc(S("gain"), 16)
            eng.wait_ge(S("sfin"), 2)
            d(T["o_dp"], S2.rearrange("p a b -> p (a b)")).then_inc(S("out"), 16)
            d(T["o_ds"], S0.rearrange("p a b -> p (a b)")).then_inc(S("out"), 16)
            eng.wait_ge(S("h_last"), 1)
            d(T["o_h"], hlast).then_inc(S("out"), 16)
            stream(B_Q0 + WSLOTS, B_QKV + WSLOTS)
            eng.wait_ge(S("Hn"), 6)
            d(gB[:, :], T["gains"][2:3, :].to_broadcast([128, D])).then_inc(S("gain"), 16)
            eng.wait_ge(S("x_new"), 6)
            d(KC.rearrange("p a b -> p (a b)"), T["kc"]).then_inc(S("kc"), 16)
            d(VC.rearrange("p a b -> p (a b)"), T["vc"]).then_inc(S("vc"), 16)
            d(lq.rearrange("p a b -> p (a b)"), T["lq"].to_broadcast([128, 256])).then_inc(S("lq"), 16)
            stream(B_QKV + WSLOTS, B_OUT1 + WSLOTS)
            eng.wait_ge(S("Hn"), 9)
            d(gB[:, :], T["gains"][3:4, :].to_broadcast([128, D])).then_inc(S("gain"), 16)
            eng.wait_ge(S("ev1"), 16)
            d(T["o_k"], KTt.rearrange("p a b -> p (a b)")).then_inc(S("out"), 16)
            eng.wait_ge(S("ev1"), 24)
            d(T["o_v"], Vt.rearrange("p a b -> p (a b)")).then_inc(S("out"), 16)
            stream(B_OUT1 + WSLOTS, NBLK)
            eng.wait_ge(S("Hn"), 12)
            d(gB[:, :], T["gains"][4:5, :].to_broadcast([128, D])).then_inc(S("gain"), 16)
            for i, t in enumerate(TILES[4]):
                eng.wait_ge(S("Hn"), 12 + i + 1)
                d(T["o_y"][:, t, :], Hn[:, t, :]).then_inc(S("out"), 16)
            if DEBUG:
                d(T["dbg"], X[:, :, :]).then_inc(S("out"), 16)
            eng.wait_ge(S("out"), 16 * (9 + DEBUG))

        @block.gpsimd
        def _(eng):
            g = nc.gpsimd
            ch = Chain(eng, "pool_own")
            for m, v in ((ident, 0.0), (ones, 1.0), (bm16, 1.0), (bm32, 1.0), (bm64, 1.0), (mhalf, -0.5), (ZR, 0.0)):
                ch.add(g.memset(m[:, :], v))
            ch.add(g.memset(RP[:, :], 0.0))
            for v in (MDT, MDs, ):
                ch.add(g.memset(v, 0.0))
            ch.add(g.memset(LTp, 1.0))
            ch.add(g.memset(PJ[:, :, 0:3], 0.0))
            ch.add(g.iota(iota16[:, :], pattern=[[1, 16]], base=0, channel_multiplier=0,
                          allow_small_or_imprecise_dtypes=True))
            ch.settle()
            ch.add(g.affine_select(out=ident[:, :], in_=ident[:, :], compare_op=ALU.not_equal, fill=1.0,
                                   base=0, pattern=[[-1, 128]], channel_multiplier=1))
            for r in range(-3, 4):
                ch.link(g.affine_select(out=RP[:, :], in_=RP[:, :], compare_op=ALU.not_equal, fill=1.0,
                                        base=32 * r, pattern=[[-1, 128]], channel_multiplier=1))
            for m, n in ((bm16, 16), (bm32, 32), (bm64, 64)):
                v = m[:, :].rearrange("p (a b) -> p a b", b=n)
                ch.link(g.affine_select(out=v, in_=v, compare_op=ALU.is_ge, fill=0.0, base=0,
                                        pattern=[[-n, 128 // n], [0, n]], channel_multiplier=1))
                ch.add(g.affine_select(out=v, in_=v, compare_op=ALU.is_ge, fill=0.0, base=n - 1,
                                       pattern=[[n, 128 // n], [0, n]], channel_multiplier=-1))
            ch.add(g.affine_select(out=LTp, in_=LTp, compare_op=ALU.is_ge, fill=0.0, base=0,
                                   pattern=[[1, 128]], channel_multiplier=-1))
            ch.add(g.affine_select(out=MDT, in_=MDT, compare_op=ALU.is_ge, fill=NEG, base=0,
                                   pattern=[[1, 128]], channel_multiplier=-1))
            ch.add(g.affine_select(out=MDs, in_=MDs, compare_op=ALU.is_ge, fill=NEG, base=-1,
                                   pattern=[[-1, 128]], channel_multiplier=1))
            ch.settle()
            ch.add(g.tensor_tensor(LTs, LTp, bm32[:, :], ALU.mult))
            for o, m in ((MDTs, MDT), (MDss, MDs)):
                o3, m3 = (v.rearrange("p (a b) -> p a b", b=32) for v in (o, m))
                ch.link(g.affine_select(out=o3, in_=m3, compare_op=ALU.is_ge, fill=NEG, base=0,
                                        pattern=[[-32, 4], [0, 32]], channel_multiplier=1))
                ch.link(g.affine_select(out=o3, in_=o3, compare_op=ALU.is_ge, fill=NEG, base=31,
                                        pattern=[[32, 4], [0, 32]], channel_multiplier=-1))
            ch.settle()
            eng.wait_ge(S("par"), 16 * 6)
            g.tensor_copy(PJ[:, :, 259:262], CSi).then_inc(S("consts"), 1)

            def norm(n):
                for i, t in enumerate(TILES[n]):
                    eng.wait_ge(S("sumsq"), 3 * n + i + 1)
                    ch.link(g.tensor_scalar(ss[:, t:t + 1], ss[:, t:t + 1], 1.0 / D, EPS, ALU.mult, ALU.add))
                    g.tensor_tensor(rstd[:, t:t + 1], ss[:, t:t + 1], mhalf[:, 0:1], ALU.pow)\
                        .then_inc(S("rstd"), 1)

            norm(0)
            for i in range(8):
                eng.wait_ge(S("silu"), i + 1)
                g.tensor_tensor(RN[:, i, :], QK[:, i, :], QK[:, i, :], ALU.mult).then_inc(S("qk_sq"), 1)
            eng.wait_ge(S("conv"), 16)
            g.tensor_copy(CSo[:, :, 0:3], PJ[:, :, 256:259]).then_inc(S("cso"), 1)
            g.tensor_copy(CSo[:, :, 3:6], PJ[:, :, 291:294]).then_inc(S("cso"), 1)
            eng.wait_ge(S("softplus"), 1)
            for f in range(4):
                eng.wait_ge(S("gate_th"), f + 1)
                g.tensor_scalar(L1[:, f, :], L1[:, f, :], 1.0, CLM[:, f:f + 1], ALU.add, ALU.mult)\
                    .then_inc(S("log_a"), 1)
            eng.wait_ge(S("lru_t"), 1)
            g.tensor_scalar(L1, L4, -1.0, 1.0, ALU.mult, ALU.add).then_inc(S("lru_den"), 1)
            eng.wait_ge(S("lru_rec"), 1)
            g.tensor_tensor(L4, L4, L1, ALU.mult).then_inc(S("lru_q"), 1)
            eng.wait_ge(S("gate_th"), 8)
            ch.link(g.tensor_scalar(L2, L2, 1.0, None, ALU.add, ALU.bypass))
            ch.link(g.tensor_tensor(L2, L2, CV[:, 12:16, :], ALU.mult))
            eng.wait_ge(S("lru_sq"), 1)
            g.tensor_tensor(L2, L2, L4, ALU.mult).then_inc(S("lru_u"), 1)
            for bt, (u0, u1) in enumerate(BT):
                eng.wait_ge(S("expE"), bt + 1)
                eng.wait_ge(S("qu"), 8)
                eng.wait_ge(S("egl"), bt + 1)
                g.tensor_tensor(E[:, u0:u1, :], E[:, u0:u1, :], QU[:, u0:u1, :], ALU.mult).then_inc(S("qe"), 1)
            eng.wait_ge(S("l2_sqrt"), 8)
            eng.wait_ge(S("qu"), 8)
            for k, (m1, m0) in enumerate(((bm32, bm16), (bm64, bm32), (ones, bm64))):
                ch.add(g.tensor_tensor(XM[:, k, :], m1[:, :], m0[:, :], ALU.subtract))
            ch.settle()
            for bt, (u0, u1) in enumerate(BT):
                n = u1 - u0
                eng.wait_ge(S("at"), bt + 1)
                for k, o in enumerate((B1T, B2T, B3T)):
                    r = g.tensor_tensor(o[:, u0:u1, :], AT_[:, u0:u1, :],
                                        XM[:, k:k + 1, :].to_broadcast([128, n, 128]), ALU.mult)
                r.then_inc(S("bmT"), 1)
            for bt, (u0, u1) in enumerate(BT):
                eng.wait_ge(S("o_ss"), u1)
                ch.link(g.tensor_scalar(ss[:, u0:u1], ss[:, u0:u1], 1.0 / 128, EPS, ALU.mult, ALU.add))
                g.tensor_tensor(rstd[:, u0:u1], ss[:, u0:u1], mhalf[:, u0:u1], ALU.pow).then_inc(S("o_rs"), 1)
            eng.wait_ge(S("hs"), 1)
            hl = hlast.rearrange("p (a b) -> p a b", b=2)
            g.tensor_copy(hl[:, :, 0:1], L1[:, :, 255:256])
            g.tensor_copy(hl[:, :, 1:2], L1[:, :, 290:291]).then_inc(S("h_last"), 1)
            g.tensor_tensor(mixT[:, 4:8, 0:NP], L1[:, :, 0:NP], GG[:, :, 0:NP], ALU.mult)
            for j in range(4):
                r = g.tensor_tensor(mixT[:, 4:8, NP + 32 * j:NP + 32 * j + 32], L1[:, :, 259:291],
                                    GG[:, :, NP:NT], ALU.mult)
            r.then_inc(S("mix_lru"), 1)
            norm(1)

            def peer(l):
                def gather(cols_, half, refill):
                    g.tensor_copy(idst[:, 8 * half:8 * half + 8], cols_).then_inc(S("staged"), 1)
                    eng.wait_ge(S("staged"), 1)
                    eng.sem_clear(S("staged"))
                    for s in range(UVS):
                        if refill:
                            eng.wait_ge(S(f"uv_free{s}"), 1)
                            eng.sem_clear(S(f"uv_free{s}"))
                        g.indirect_dma_start(UV[:, s, :], None, T[f"uv{l}"], bass.IndirectOffsetOnAxis(
                            ap=idst[:, 8 * half + s:8 * half + s + 1], axis=0)).then_inc(S(f"uv_in{s}"), 16)

                for un, (c0, n) in enumerate(((256, 2), (0, 8), (128, 8))):
                    if un == 0:
                        for gq in range(2):
                            eng.wait_ge(S("idx"), 18 * l + 5 + 4 * gq)
                            for half in range(2):
                                c = c0 + 16 * gq + 8 * half
                                gather(idx[:, c:c + 8], half, l or gq or half)
                        continue
                    eng.wait_ge(S("idx"), 18 * l + (10, 18)[un - 1])
                    with eng.Fori(0, n) as i:
                        for half in range(2):
                            gather(idx[:, bass.ds(i * 16 + (c0 + 8 * half), 8)], half, True)

            peer(0)
            norm(2)
            eng.wait_ge(S("x_new"), 6)
            ch.add(g.memset(QZ, 0.0))
            ch.link(g.memset(msk, 0.0))
            for o in (64, 320):
                r = g.affine_select(out=msk[:, o:o + 64], in_=msk[:, o:o + 64], compare_op=ALU.is_ge, fill=NEG,
                                    base=-64, pattern=[[0, 64]], channel_multiplier=1)
            r.then_inc(S("l1_consts"), 1)
            eng.wait_ge(S("os_ss"), 1)
            ch.link(g.tensor_scalar(ss[:, :], ss[:, :], 1.0 / 128, EPS, ALU.mult, ALU.add))
            g.tensor_tensor(rstd[:, :], ss[:, :], mhalf[:, :], ALU.pow).then_inc(S("os_rs"), 1)
            norm(3)
            peer(1)
            norm(4)

        @block.scalar
        def _(eng):
            s = nc.scalar
            ch = Chain(eng, "act_own")
            d = s.dma_start
            par = S("par")
            d(cols[:, :], T["cols"]).then_inc(par, 16)
            d(CSi.rearrange("p a b -> p (a b)"), T["st_conv"]).then_inc(par, 16)
            d(WBA.rearrange("p a b -> p (a b)"), T["wba"]).then_inc(par, 16)
            d(keysT[:, :, :, :].rearrange("p a b c -> p (a b c)"), T["keys"]).then_inc(par, 16)
            d(GW.rearrange("p a b c -> p (a b c)"), T["gw"]).then_inc(par, 16)
            d(S0.rearrange("p a b -> p (a b)"), T["s0"]).then_inc(par, 16)

            def squares(n):
                for i, t in enumerate(TILES[n]):
                    if n == 0:
                        eng.wait_ge(S(f"x_in{t}"), 16)
                    else:
                        eng.wait_ge(S("x_new"), 3 * (n - 1) + i + 1)
                    if n or i:
                        eng.wait_ge(S("sumsq"), 3 * n + i)
                    if n >= 1 and i == 0:
                        eng.wait_ge(S("rstd"), 3 * n)
                    junk = 2 if n in (2, 4) and i < 2 else 6
                    s.activation(PS[:, junk:junk + 2, :], X[:, t, :].rearrange("p (a b) -> p a b", b=512), ACT.Square,
                                 accum_out=ss[:, t:t + 1]).then_inc(S("sumsq"), 1)

            def evac_hT(n):
                for i, t in enumerate(TILES[n]):
                    eng.wait_ge(S("tr"), 3 * n + i + 1)
                    s.activation(hT[:, 0:4, 128 * t:128 * t + 128],
                                 PS[:, 2 * t, :].rearrange("p (a b) -> p a b", b=128), ACT.Copy).then_inc(S("hT_a"), 1)

            squares(0)
            eng.wait_ge(par, 16 * 6)
            evac_hT(0)

            def post_conv(bb):
                eng.wait_ge(S("conv"), bb + 1)
                if bb < 8:
                    s.activation(QK[:, bb, :], CV[:, bb, :], ACT.Silu).then_inc(S("silu"), 1)
                else:
                    h = bb - 8
                    ch.add(s.activation(VU[:, h:h + 5:4, :], CV[:, bb, 0:NP].rearrange("p (a b) -> p a b", b=128),
                                 ACT.Silu))
                    s.activation(VU[:, 8, 32 * h:32 * h + 32], CV[:, bb, 259:291], ACT.Silu).then_inc(S("silu"), 1)

            for bb in range(24):
                eng.wait_ge(S("blk"), bb + 1)
                bank = PS[:, bb % 4, :]
                if bb < 12 or 16 <= bb < 20:
                    f = bb if bb < 12 else bb - 4
                    ch.add(s.activation(PJ[:, f, 3:259], bank[:, 0:NP], ACT.Copy))
                    s.activation(PJ[:, f, 262:294], bank[:, NP:NT], ACT.Copy).then_inc(S("ev0"), 1)
                elif bb < 16:
                    s.activation(SZ[:, bb - 12, :], bank[:, 0:NT], ACT.Silu).then_inc(S("ev0"), 1)
                else:
                    s.activation(GG[:, bb - 20, :], bank[:, 0:NT], ACT.Gelu_apprx_tanh).then_inc(S("ev0"), 1)
                if 2 <= bb < 14:
                    post_conv(bb - 2)
                if bb in (16, 17):
                    for i in range(4 * (bb - 16), 4 * (bb - 16) + 4):
                        eng.wait_ge(S("l2"), i + 1)
                        sc = 128.0 if i < 4 else 1.0
                        s.activation(RN[:, i, :], PS[:, 4 + i % 4, 0:291], ACT.Sqrt, bias=sc * EPS, scale=sc)\
                            .then_inc(S("l2_sqrt"), 1)
            eng.wait_ge(S("ba"), 1)
            ch.add(s.activation(TH[:, 0:9], BE, ACT.Tanh, scale=0.5))
            ch.add(s.activation(EAL, cols[:, C_AL:C_AL + 9], ACT.Exp))
            s.activation(EX, MN, ACT.Exp).then_inc(S("ba_exp"), 1)
            for i in range(8):
                gt, f = i // 4, i % 4
                eng.wait_ge(S("gmm"), i + 1)
                eng.wait_ge(S("half_b"), 1)
                o = (L1, L2)[gt]
                s.activation(o[:, f, :], PS[:, 4 + i % 2, 0:291], ACT.Tanh, scale=0.5,
                             bias=HB[:, i:i + 1]).then_inc(S("gate_th"), 1)
            eng.wait_ge(S("log_a"), 4)
            ch.add(s.activation(L3, L1, ACT.Exp))
            s.activation(L4, L1, ACT.Tanh).then_inc(S("lru_t"), 1)
            for bt, (u0, u1) in enumerate(BT):
                n = u1 - u0
                eng.wait_ge(S("tds"), bt + 1)
                gcb = PS[:, (0, 3, 6)[bt], 0:128 * n].rearrange("p (a b) -> p a b", b=128)
                s.activation(E[:, u0:u1, :], gcb, ACT.Exp).then_inc(S("expE"), 1)
                if bt == 0:
                    eng.wait_ge(S("gc"), 1)
                    s.activation(EGC, GC, ACT.Exp).then_inc(S("egc"), 1)
                for u in range(u0, u1):
                    ch.add(s.activation(DT[:, u, :], TD[:, u, :], ACT.Exp, bias=NGC[:, u:u + 1]))
                    s.activation(Dm[:, u, :], TS[:, u, :], ACT.Exp, bias=GC[:, u:u + 1]).then_inc(S("expD"), 1)
            eng.wait_ge(S("lru_q"), 1)
            s.activation(L4, L4, ACT.Sqrt, scale=-0.5).then_inc(S("lru_sq"), 1)
            for bt, (u0, u1) in enumerate(BT):
                n = u1 - u0
                eng.wait_ge(S("at_mm"), bt + 1)
                s.activation(AT_[:, u0:u1, :], PS[:, (1, 4, 7)[bt], 0:128 * n].rearrange("p (a b) -> p a b", b=128),
                             ACT.Copy).then_inc(S("at"), 1)
            for bt, (u0, u1) in enumerate(BT):
                eng.wait_ge(S("kv_tr"), bt + 1)
                eng.wait_ge(S("aq"), 3)
                kb, vb = ((0, 2), (3, 5), (6, 6))[bt]
                for u in range(u0, u1):
                    c = 128 * (u - u0)
                    cv = c if bt < 2 else 128
                    ch.add(s.activation(KBE[:, u, :], PS[:, kb, c:c + 128], ACT.Copy, scale=BEG[:, u:u + 1]))
                    s.activation(BV[:, u, :], PS[:, vb, cv:cv + 128], ACT.Copy, scale=BE[:, u:u + 1])\
                        .then_inc(S("kbe"), 1)
            for st, name in enumerate(INV):
                for bt, (u0, u1) in enumerate(BT):
                    n = u1 - u0
                    if not INV_A[name]:
                        continue
                    eng.wait_ge(S("inv_mm"), 3 * st + bt + 1)
                    bk = (0, 4, 0)[bt]

                    def cp(dst, i):
                        return s.activation(dst[:, u0:u1, :], PS[:, bk + i, 0:128 * n]
                                            .rearrange("p (a b) -> p a b", b=128), ACT.Copy)
                    if name == "a2":
                        cp(P2, 0).then_inc(S("inv_a"), 1)
                    elif name == "n2":
                        ch.add(cp(P4, 2))
                        cp(P4T, 3).then_inc(S("inv_a"), 1)
                    elif name == "n4":
                        cp(P8T, 2).then_inc(S("inv_a"), 1)
                    else:
                        cp(XM, 0).then_inc(S("inv_a"), 1)
            for bt, (u0, u1) in enumerate(BT):
                n = u1 - u0
                eng.wait_ge(S("w_mm"), bt + 1)
                s.activation(NW[:, u0:u1, :], PS[:, (0, 4, 1)[bt], 0:128 * n].rearrange("p (a b) -> p a b", b=128),
                             ACT.Copy, scale=-1.0).then_inc(S("nw"), 1)
            for bt, bk in ((0, 2), (2, 3), (1, 5)):
                u0, u1 = BT[bt]
                n = u1 - u0
                eng.wait_ge(S("vn_mm"), (0, 2, 1)[bt] + 1)
                if bt == 2:
                    for h in range(4):
                        s.activation(VNm[:, h, :], PS[:, bk, 0:128], ACT.Copy, scale=bm32[:, 32 * h:32 * h + 1])
                s.activation(VN[:, u0:u1, :], PS[:, bk, 0:128 * n].rearrange("p (a b) -> p a b", b=128),
                             ACT.Copy).then_inc(S("vn"), 1)
            for bt, (u0, u1) in enumerate(BT):
                eng.wait_ge(S("o_mm"), (1, 3, 2)[bt])
                for u in range(u0, u1):
                    s.activation(TD[:, u, :], PS[:, (6, 1, 7)[bt], 128 * (u - u0):128 * (u - u0) + 128], ACT.Square,
                                 accum_out=ss[:, u:u + 1]).then_inc(S("o_ss"), 1)
            squares(1)
            evac_hT(1)

            def peer(l):
                def score(j):
                    eng.wait_ge(S("sc_mm"), 16 * l + j + 1)
                    bk = PS[:, j % 4, :]
                    h, pt = j // 2, j % 2
                    q = 32 * (h % 4)
                    ch.add(s.activation(SC.rearrange("p (t m) n -> p t m n", t=2)[:, :, j, :],
                                 bk[:, 0:256].rearrange("p (t n) -> p t n", t=2), ACT.Copy))
                    s.activation(SCS[q:q + 32, 2 * (h // 4) + pt, :], bk[q:q + 32, 256:384], ACT.Copy)\
                        .then_inc(S("sc"), 1)
                bq = (B_Q0, B_Q1)[l]
                for j in range(16):
                    eng.wait_ge(S("blk"), bq + j + 1)
                    s.activation(QT[:, j % 4, :], PS[:, 4 + j % 2, 0:NT], ACT.Copy).then_inc(S("qt"), 1)
                    if j >= 1:
                        score(j - 1)
                score(15)

                def gate_exp(un):
                    eng.wait_ge(S("gmax"), 3 * l + un + 1)
                    c0, nh = ((256, 2), (0, 8), (128, 8))[un]
                    s.activation(gate[:, c0:c0 + 16 * nh], gate[:, c0:c0 + 16 * nh], ACT.Exp).then_inc(S("gexp"), 1)

                gate_exp(0)
                gate_exp(1)
                base = 288 * l
                for un, n in enumerate((2, 8, 8)):
                    if un == 2:
                        gate_exp(2)
                    with eng.Fori(0, n) as i:
                        for c in range(16):
                            eng.wait_ge(S("dots"), i * 16 + (base + c + 1))
                            o = c % UVS
                            s.activation(gl[:, o:o + 1], dots[:, o:o + 1], ACT.Gelu_apprx_tanh).then_inc(S("gelu"), 1)
                    base += 16 * n

            peer(0)
            squares(2)
            evac_hT(2)
            eng.wait_ge(S("lam_s"), 1)
            s.activation(la_[:, 2:4], la_[:, 0:2], ACT.Exp).then_inc(S("lam_e"), 1)
            eng.wait_ge(S("l1_consts"), 1)
            for j in range(24):
                eng.wait_ge(S("blk"), B_QKV + j + 1)
                bank = PS[:, j % 4, :]
                if j < 8:
                    ch.add(s.activation(QZ[0:64, 2 * j, :], bank[0:64, 0:NT], ACT.Copy, scale=0.125))
                    s.activation(QZ[64:128, 2 * j + 1, :], bank[64:128, 0:NT], ACT.Copy, scale=0.125)\
                        .then_inc(S("ev1"), 1)
                elif j < 16:
                    s.activation(KTt[:, j - 8, :], bank[:, 0:NT], ACT.Copy).then_inc(S("ev1"), 1)
                else:
                    s.activation(Vt[:, :, 128 * (j - 16):128 * (j - 16) + 128],
                                 bank[:, 0:384].rearrange("p (t n) -> p t n", t=3), ACT.Copy).then_inc(S("ev1"), 1)
            for h in range(HC + 1):
                if h < HC:
                    q = h % 2
                    eng.wait_ge(S("smax"), h + 1)
                    for t in range(2):
                        for c in range(2):
                            w0, w1 = ((0, 128), (128, 384))[t]
                            s.activation(PP[:, q, 384 * c + w0:384 * c + w1], PS[:, 2 * q + c, w0:w1], ACT.Exp,
                                         bias=la_[:, 8 + 8 * q + 2 * t + c:9 + 8 * q + 2 * t + c],
                                         accum_out=la_[:, 24 + 8 * q + 2 * t + c:25 + 8 * q + 2 * t + c])\
                                .then_inc(S("sexp"), 1)
                if h >= 1:
                    q = (h - 1) % 2
                    eng.wait_ge(S("p_tr"), h)
                    s.activation(PTt[:, q, :], PS[:, 4 + q, 0:384], ACT.Copy).then_inc(S("pt"), 1)
            for gq in range(2):
                eng.wait_ge(S("ssmax"), gq + 1)
                for c in range(2):
                    s.activation(PPs[:, c, :], PS[:, 2 * c:2 * c + 2, :].rearrange("p a b -> p (a b)")[:, 0:544], ACT.Exp,
                                 bias=la_[:, 40 + c:41 + c], accum_out=la_[:, 44 + c:45 + c]).then_inc(S("ssexp"), 1)
                eng.wait_ge(S("ps_tr"), gq + 1)
                ch.add(s.activation(PTt.rearrange("p a b -> p (a b)")[:, 0:512], PS[:, 4, :], ACT.Copy))
                s.activation(PTt.rearrange("p a b -> p (a b)")[0:32, 512:640], PS[0:32, 5, 0:128], ACT.Copy)\
                    .then_inc(S("pts"), 1)
            eng.wait_ge(S("cn"), 1)
            for i in range(5):
                eng.wait_ge(S("o_tr"), i + 1)
                if i < 4:
                    t, hh = i // 2, i % 2
                    s.activation(mixT[:, 4 * hh:4 * hh + 4, 128 * t:128 * t + 128],
                                 PS[:, i, :].rearrange("p (a b) -> p a b", b=128), ACT.Copy,
                                 scale=la_[:, 50:51]).then_inc(S("mix1"), 1)
                else:
                    for gq in range(2):
                        for r in range(4):
                            s.activation(mixT[:, 4 * gq:4 * gq + 4, NP + 32 * r:NP + 32 * r + 32],
                                         PS[:, 4, 128 * gq:128 * gq + 128].rearrange("p (a b) -> p a b", b=32),
                                         ACT.Copy, scale=la_[:, 50:51]).then_inc(S("mix1"), 1)
            squares(3)
            evac_hT(3)
            peer(1)
            squares(4)

        @block.vector
        def _(eng):
            v = nc.vector
            ch = Chain(eng, "dve_own")

            def norm(n, last=False):
                for i, t in enumerate(TILES[n]):
                    eng.wait_ge(S("gain"), 16 * (n + 1))
                    eng.wait_ge(S("rstd"), 3 * n + i + 1)
                    v.scalar_tensor_tensor(out=Hn[:, t, :], in0=X[:, t, :], scalar=rstd[:, t:t + 1], in1=gB[:, :],
                                           op0=ALU.mult, op1=ALU.mult).then_inc(S("Hn"), 1)
                if last:
                    return
                for i, t in enumerate(TILES[n]):
                    eng.wait_ge(S("tr"), 3 * n + i + 1)
                    v.tensor_copy(hT[:, 4:8, 128 * t:128 * t + 128],
                                  PS[:, 2 * t + 1, :].rearrange("p (a b) -> p a b", b=128)).then_inc(S("hT_v"), 1)

            norm(0)
            eng.wait_ge(S("ba_mm"), 1)
            eng.wait_ge(S("par"), 16 * 6)
            ch.link(v.tensor_copy(BA, PS[:, 4, 0:24]))
            ba = BA.rearrange("p (t c) -> p t c", c=8)
            ch.add(v.tensor_copy(BE[:, 0:8].rearrange("p (t c) -> p t c", c=4), ba[:, 0:2, 0:4]))
            ch.add(v.tensor_tensor(AL[:, 0:8].rearrange("p (t c) -> p t c", c=4), ba[:, 0:2, 4:8],
                            cols[:, C_DT:C_DT + 8].rearrange("p (t c) -> p t c", c=4), ALU.add))
            for h in range(4):
                r = slice(32 * h, 32 * h + 32)
                ch.add(v.tensor_copy(BE[r, 8:9], BA[r, 16 + h:17 + h]))
                ch.add(v.tensor_tensor(AL[r, 8:9], BA[r, 20 + h:21 + h], cols[r, C_DT + 8:C_DT + 9], ALU.add))
            ch.add(v.tensor_scalar(AL[:, 9:13], cols[:, C_LM:C_LM + 4], -1.0, None, ALU.mult))
            v.tensor_scalar(HB, cols[:, C_GA:C_GA + 8], 0.5, None, ALU.mult).then_inc(S("half_b"), 1)
            ch.settle()
            ch.link(v.tensor_scalar(SR, AL, -1.0, None, ALU.mult))
            v.tensor_tensor(MN, AL, SR, ALU.min).then_inc(S("ba"), 1)

            def conv(f):
                w = lambda j: cols[:, C_CW + 4 * f + j:C_CW + 4 * f + j + 1]
                if f < 12:
                    ch.link(v.tensor_scalar(CV[:, f, :], PJ[:, f, 0:291], w(0), None, ALU.mult))
                else:
                    ch.link(v.tensor_scalar(CV[:, f, :], PJ[:, f, 0:291], w(0), cols[:, C_CB + f - 12:C_CB + f - 11],
                                            ALU.mult, ALU.add))
                for j in (1, 2):
                    ch.link(v.scalar_tensor_tensor(out=CV[:, f, :], in0=PJ[:, f, j:j + 291], scalar=w(j),
                                                   in1=CV[:, f, :], op0=ALU.mult, op1=ALU.add))
                v.scalar_tensor_tensor(out=CV[:, f, :], in0=PJ[:, f, 3:294], scalar=w(3), in1=CV[:, f, :],
                                       op0=ALU.mult, op1=ALU.add).then_inc(S("conv"), 1)

            eng.wait_ge(S("consts"), 1)
            for f in range(12):
                eng.wait_ge(S("ev0"), f + 1)
                conv(f)
            for i in range(8):
                eng.wait_ge(S("l2_sqrt"), i + 1)
                ch.link(v.reciprocal(RN[:, i, :], RN[:, i, :]))
                o, h = (QU, KU)[i // 4], i % 4
                two = lambda t: t[:, i, 0:NP].rearrange("p (a b) -> p a b", b=128)
                ch.add(v.tensor_tensor(o[:, h:h + 5:4, :], two(QK), two(RN), ALU.mult))
                v.tensor_tensor(o[:, 8, 32 * h:32 * h + 32], QK[:, i, 259:291], RN[:, i, 259:291], ALU.mult)\
                    .then_inc(S("qu"), 1)
            for f in range(12, 16):
                eng.wait_ge(S("ev0"), f + 4 + 1)
                conv(f)
            eng.wait_ge(S("ba_exp"), 1)
            ch.link(v.tensor_scalar(SR, EX, 2.0, None, ALU.add))
            ch.link(v.reciprocal(SR, SR))
            ch.link(v.tensor_tensor(SR, SR, EX, ALU.mult))
            ch.link(v.tensor_tensor(SQ_, SR, SR, ALU.mult))
            ch.link(v.tensor_scalar(PL, SQ_, 1.0 / 17, None, ALU.mult))
            for k in (15, 13, 11, 9, 7, 5, 3):
                ch.link(v.scalar_tensor_tensor(out=PL, in0=PL, scalar=1.0 / k, in1=SQ_, op0=ALU.add, op1=ALU.mult))
            ch.link(v.scalar_tensor_tensor(out=PL, in0=PL, scalar=1.0, in1=SR, op0=ALU.add, op1=ALU.mult))
            ch.link(v.tensor_scalar(SP, AL, 0.0, None, ALU.max))
            ch.link(v.scalar_tensor_tensor(out=SP, in0=PL, scalar=2.0, in1=SP, op0=ALU.mult, op1=ALU.add))
            ch.add(v.tensor_scalar(CLM, SP[:, 9:13], -4.0, None, ALU.mult))
            ch.add(v.tensor_scalar(BE, TH[:, 0:9], 0.5, 0.5, ALU.mult, ALU.add))
            v.scalar_tensor_tensor(out=G9, in0=SP[:, 0:9], scalar=-1.0, in1=EAL, op0=ALU.mult, op1=ALU.mult)\
                .then_inc(S("softplus"), 1)
            eng.wait_ge(S("gc_mm"), 1)
            ch.link(v.tensor_copy(GC, PS[:, 7, 0:9]))
            v.tensor_scalar(NGC, GC, -1.0, None, ALU.mult).then_inc(S("gc"), 1)
            for bt, (u0, u1) in enumerate(BT):
                n = u1 - u0
                if bt < 2:
                    eng.wait_ge(S("gcB"), bt + 1)
                else:
                    eng.wait_ge(S("kk"), 3)
                gcb = PS[:, (0, 3, 6)[bt], 0:128 * n].rearrange("p (a b) -> p a b", b=128)
                mt, ms = ((MDT, MDs), (MDT, MDs), (MDTs, MDss))[bt]
                bc = lambda m: m.unsqueeze(1).to_broadcast([128, n, 128])
                ch.add(v.tensor_tensor(TD[:, u0:u1, :], gcb, bc(mt), ALU.add))
                v.scalar_tensor_tensor(out=TS[:, u0:u1, :], in0=gcb, scalar=-1.0, in1=bc(ms), op0=ALU.mult,
                                       op1=ALU.add).then_inc(S("tds"), 1)
            eng.wait_ge(S("egc"), 1)
            ch.link(v.tensor_tensor(BEG, BE, EGC, ALU.mult))
            eng.wait_ge(S("lru_den"), 1)
            v.reciprocal(L1, L1).then_inc(S("lru_rec"), 1)
            for bt, (u0, u1) in enumerate(BT):
                n = u1 - u0
                eng.wait_ge(S("expE"), bt + 1)
                eng.wait_ge(S("expD"), u1)
                if bt < 2:
                    ch.add(v.tensor_copy(EGL[:, u0:u1], E[:, u0:u1, 127:128].rearrange("p a b -> p (a b)")))
                    r = v.tensor_copy(DEC[:, u0:u1], DT[:, u0:u1, 127:128].rearrange("p a b -> p (a b)"))
                else:
                    ch.add(v.tensor_copy(egls, E[:, 8, 31:128:32]))
                    r = v.tensor_reduce(DEC[:, 8:9], DT[:, 8, 31:128:32], AX.X, ALU.add)
                r.then_inc(S("egl"), 1)
                kk = PS[:, (1, 4, 6)[bt], :]
                c0 = (0, 0, 128)[bt]
                eng.wait_ge(S("kk"), bt + 1)
                for u in range(u0, u1):
                    c = c0 + 128 * (u - u0)
                    v.scalar_tensor_tensor(out=Am[:, u, :], in0=kk[:, c:c + 128], scalar=BE[:, u:u + 1],
                                           in1=Dm[:, u, :], op0=ALU.mult, op1=ALU.mult).then_inc(S("A"), 1)
                qk = PS[:, (2, 5, 6)[bt], :]
                eng.wait_ge(S("egl"), bt + 1)
                c0 = (0, 0, 256)[bt]
                v.tensor_tensor(DT[:, u0:u1, :], qk[:, c0:c0 + 128 * n].rearrange("p (a b) -> p a b", b=128),
                                DT[:, u0:u1, :], ALU.mult).then_inc(S("aq"), 1)
            eng.wait_ge(S("egl"), 3)
            for bt, (u0, u1) in enumerate(BT):
                n = u1 - u0
                eng.wait_ge(S("kv_tr"), bt + 1)
                kb = (0, 3, 6)[bt]
                eng.wait_ge(S("kbe"), u1)
                ch.add(v.tensor_tensor(KDEC[:, u0:u1, :], PS[:, kb, 0:128 * n].rearrange("p (a b) -> p a b", b=128),
                                DEC[:, u0:u1].unsqueeze(2).to_broadcast([128, n, 128]), ALU.mult))
                bc = lambda m: m[:, :].unsqueeze(1).to_broadcast([128, n, 128])
                eng.wait_ge(S("at"), bt + 1)
                ch.add(v.tensor_tensor(P1[:, u0:u1, :], Am[:, u0:u1, :], bc(bm16), ALU.mult))
                ch.link(v.tensor_tensor(P1T[:, u0:u1, :], AT_[:, u0:u1, :], bc(bm16), ALU.mult))
                ch.add(v.scalar_tensor_tensor(out=Tm[:, u0:u1, :], in0=P1[:, u0:u1, :], scalar=-1.0, in1=bc(ident),
                                       op0=ALU.mult, op1=ALU.add))
                v.scalar_tensor_tensor(out=TTm[:, u0:u1, :], in0=P1T[:, u0:u1, :], scalar=-1.0, in1=bc(ident),
                                       op0=ALU.mult, op1=ALU.add).then_inc(S("t0"), 1)
            for st, name in enumerate(INV):
                for bt, (u0, u1) in enumerate(BT):
                    n = u1 - u0
                    if not INV_V[name]:
                        continue
                    eng.wait_ge(S("inv_mm"), 3 * st + bt + 1)
                    bk = (0, 4, 0)[bt]
                    src = lambda i: PS[:, bk + i, 0:128 * n].rearrange("p (a b) -> p a b", b=128)
                    if name == "a2":
                        v.tensor_copy(P2T[:, u0:u1, :], src(1)).then_inc(S("inv_v"), 1)
                        continue
                    op = ALU.add if name[0] == "n" else ALU.subtract
                    if name != "m3":
                        ch.add(v.tensor_tensor(Tm[:, u0:u1, :], Tm[:, u0:u1, :], src(0), op))
                    v.tensor_tensor(TTm[:, u0:u1, :], TTm[:, u0:u1, :], src(1), op).then_inc(S("inv_v"), 1)
            eng.wait_ge(S("s_mm"), 1)
            v.tensor_copy(S1, PS[:, 4, :].rearrange("p (a b) -> p a b", b=128)).then_inc(S("s1"), 1)
            eng.wait_ge(S("s_mm"), 2)
            for h in range(4):
                r = v.scalar_tensor_tensor(out=S0[:, h, :], in0=S0[:, h, :], scalar=egls[:, h:h + 1],
                                           in1=PS[:, 0, 128 * h:128 * h + 128], op0=ALU.mult, op1=ALU.add)
            r.then_inc(S("sfin"), 1)
            eng.wait_ge(S("s_mm"), 3)
            for h in range(4):
                r = v.scalar_tensor_tensor(out=S2[:, h, :], in0=S1[:, h, :], scalar=EGL[:, 4 + h:5 + h],
                                           in1=PS[:, 4, 128 * h:128 * h + 128], op0=ALU.mult, op1=ALU.add)
            r.then_inc(S("sfin"), 1)
            eng.wait_ge(S("lru_u"), 1)
            for f in range(4):
                ch.add(v.tensor_tensor_scan(L1[:, f, 0:NP], L3[:, f, 0:NP], L2[:, f, 0:NP], 0.0, ALU.mult, ALU.add))
                r = v.tensor_tensor_scan(L1[:, f, 259:291], L3[:, f, 259:291], L2[:, f, 259:291],
                                         cols[:, C_H0 + f:C_H0 + f + 1], ALU.mult, ALU.add)
            r.then_inc(S("hs"), 1)
            for bt, (u0, u1) in enumerate(BT):
                n = u1 - u0
                eng.wait_ge(S("o_rs"), bt + 1)
                v.tensor_tensor(ON[:, u0:u1, :], PS[:, (6, 1, 7)[bt], 0:128 * n].rearrange("p (a b) -> p a b", b=128),
                                rstd[:, u0:u1].unsqueeze(2).to_broadcast([128, n, 128]), ALU.mult)\
                    .then_inc(S("on"), 1)
            for bt, (u0, u1) in enumerate(BT):
                eng.wait_ge(S("on_tr"), bt + 1)
                if bt < 2:
                    ch.add(v.scalar_tensor_tensor(out=mixT[:, 0:4, 128 * bt:128 * bt + 128],
                                           in0=PS[:, (2, 3)[bt], :].rearrange("p (a b) -> p a b", b=128),
                                           scalar=cols[:, C_AN:C_AN + 1], in1=SZ[:, :, 128 * bt:128 * bt + 128],
                                           op0=ALU.mult, op1=ALU.mult))
                else:
                    for r in range(4):
                        last = v.scalar_tensor_tensor(out=mixT[:, 0:4, NP + 32 * r:NP + 32 * r + 32],
                                                      in0=PS[:, 5, 0:128].rearrange("p (a b) -> p a b", b=32),
                                                      scalar=cols[:, C_AN:C_AN + 1], in1=SZ[:, :, NP:NT],
                                                      op0=ALU.mult, op1=ALU.mult)
            last.then_inc(S("mix_d"), 1)

            def residual(l):
                for half in range(2):
                    eng.wait_ge(S("blk"), (B_OUT0, B_OUT1)[l] + 4 * half + 4)
                    for t in range(3):
                        o = X[:, t, 512 * half:512 * half + 512]
                        r = v.tensor_tensor(o, o, PS[:, 2 * t + half, :], ALU.add)
                        if half:
                            r.then_inc(S("x_new"), 1)
                        else:
                            ch.add(r)
                ch.settle()

            residual(0)
            norm(1)

            def top16(n, src, tmp, val, ind):
                for i in range(n):
                    ch.add(v.max(val(i)[:, 0:8], src(i)))
                ch.settle()
                for i in range(n):
                    ch.add(v.max_index(ind(i)[:, 0:8], val(i)[:, 0:8], src(i)))
                    ch.add(v.match_replace(tmp(i), val(i)[:, 0:8], src(i), -3.0e38))
                ch.settle()
                for i in range(n):
                    ch.add(v.max(val(i)[:, 8:16], tmp(i)))
                ch.settle()
                for i in range(n):
                    ch.add(v.max_index(ind(i)[:, 8:16], val(i)[:, 8:16], tmp(i)))

            def pick(sc, idx_to, gate_to):
                top16(2, lambda c: sc[:, c, :], lambda c: tm[:, c, :], lambda c: pv_[:, c, :], lambda c: pi[:, c, :])
                ch.settle()
                ch.link(v.tensor_tensor(cand, pv_[:, 0, :].unsqueeze(2).to_broadcast([128, 16, 16]),
                                        pv_[:, 1, :].unsqueeze(1).to_broadcast([128, 16, 16]), ALU.add))
                flat = cand.rearrange("p a b -> p (a b)")
                top16(1, lambda i: flat, lambda i: candt, lambda i: tv, lambda i: sel)
                ch.settle()
                ch.add(v.tensor_copy(gate_to, tv))
                ch.add(v.tensor_scalar(ab[:, 0:16], sel, 4, None, ALU.logical_shift_right))
                ch.link(v.tensor_scalar(ab[:, 16:32], sel, 15, None, ALU.bitwise_and))
                ch.link(v.tensor_tensor(hot, ab.unsqueeze(2).to_broadcast([128, 32, 16]),
                                        iota16[:, :].unsqueeze(1).to_broadcast([128, 32, 16]), ALU.is_equal))
                h4 = hot.rearrange("p (c k) n -> p c k n", c=2)
                ch.link(v.tensor_tensor(h4, h4, pi.unsqueeze(2).to_broadcast([128, 2, 16, 16]), ALU.mult))
                ch.link(v.tensor_reduce(i12, hot, AX.X, ALU.add))
                v.scalar_tensor_tensor(out=idx_to, in0=i12[:, 0:16], scalar=float(NKEY), in1=i12[:, 16:32],
                                       op0=ALU.mult, op1=ALU.add).then_inc(S("idx"), 1)

            def gate_of(l, un):
                c0, nh = ((256, 2), (0, 8), (128, 8))[un]
                ch.settle()
                gt = gate[:, c0:c0 + 16 * nh].rearrange("p (h s) -> p h s", s=16)
                top = gsum[:, 0:nh].unsqueeze(2)
                ch.link(v.tensor_copy(top, gt[:, :, 0:1]))
                v.tensor_tensor(gt, gt, top.to_broadcast([128, nh, 16]), ALU.subtract).then_inc(S("gmax"), 1)
                eng.wait_ge(S("gexp"), 3 * l + un + 1)
                ch.link(v.tensor_reduce(gsum[:, 0:nh], gt, AX.X, ALU.add))
                ch.link(v.reciprocal(gsum[:, 0:nh], gsum[:, 0:nh]))
                ch.link(v.tensor_tensor(gt, gt, top.to_broadcast([128, nh, 16]), ALU.mult))

            def peer(l):
                SCf = SC.rearrange("p a b -> p (a b)")

                def pick_tile0(h):
                    eng.wait_ge(S("sc"), 16 * l + 2 * h + 2)
                    pick(SC[:, 2 * h:2 * h + 2, :], idx[:, 16 * h:16 * h + 16], gate[:, 16 * h:16 * h + 16])

                def pick_sample(gq):
                    eng.wait_ge(S("sc"), 16 * l + 8 * gq + 8)
                    c = 256 + 16 * gq
                    pick(SCS[:, 2 * gq:2 * gq + 2, :], idx[:, c:c + 16], gate[:, c:c + 16])

                for h in range(PH):
                    if h in (4, 7):
                        pick_sample(h // 7)
                    pick_tile0(h)
                gate_of(l, 0)
                gate_of(l, 1)
                base = 288 * l
                for un, (c0, n) in enumerate(((256, 2), (0, 8), (128, 8))):
                    xt = (2, 0, 1)[un]
                    if un == 2:
                        gate_of(l, 2)
                    with eng.Fori(0, n) as i:
                        if un == 1:
                            ch.loop()
                            ch.link(v.tensor_copy(rows.rearrange("p a b -> p (a b)"),
                                                  SCf[:, bass.ds(i * 2 * NKEY + 16 * NKEY, 2 * NKEY)]))
                            pick(rows, idx[:, bass.ds(i * 16 + 128, 16)], gate[:, bass.ds(i * 16 + 128, 16)])
                            ch.loop_end()
                        v.tensor_copy(gst[:, :], gate[:, bass.ds(i * 16 + c0, 16)]).then_inc(S("gates"), 1)
                        eng.wait_ge(S("gates"), i + (base // 16 + 1))
                        for c in range(16):
                            sl = c % UVS
                            eng.wait_ge(S(f"uv_in{sl}"), i * 32 + 16 * (base // UVS + c // UVS + 1))
                            v.tensor_tensor_reduce(UV[:, sl, 0:D], UV[:, sl, 0:D], Hn[:, xt, :], 1.0, 0.0,
                                                   ALU.mult, ALU.add, dots[:, sl:sl + 1]).then_inc(S("dots"), 1)
                            eng.wait_ge(S("gelu"), i * 16 + (base + c + 1))
                            v.tensor_scalar(DG[:, sl, :], ident[:, :], gl[:, sl:sl + 1], gst[:, c:c + 1],
                                            ALU.mult, ALU.mult).then_inc(S("diag"), 1)
                        eng.wait_ge(S("diag"), i * 16 + (base + 16))
                    base += 16 * n
                    eng.wait_ge(S("acc"), 4 * l + (1, 3, 4)[un])
                    if un == 0:
                        for half in range(2):
                            v.tensor_copy(YS[:, 512 * half:512 * half + 512],
                                          PS[:, half, :]).then_inc(S("ys"), 1)
                        eng.wait_ge(S("acc"), 4 * l + 2)
                    for half in range(2):
                        o = X[:, xt, 512 * half:512 * half + 512]
                        r = v.tensor_tensor(o, o, PS[:, (2, 4, 6)[un] + half, :], ALU.add)
                        if half:
                            r.then_inc(S("x_new"), 1)
                        else:
                            ch.add(r)

            peer(0)
            norm(2)
            eng.wait_ge(S("lq"), 16)
            ch.link(v.tensor_tensor(lq[:, 0:2, :], lq[:, 0:2, :], lq[:, 2:4, :], ALU.mult))
            v.tensor_reduce(la_[:, 0:2], lq[:, 0:2, :], AX.X, ALU.add).then_inc(S("lam_s"), 1)
            ch.link(v.tensor_scalar(la_[:, 50:51], cols[:, C_CN:C_CN + 1], 1.0 - LAM_INIT, None, ALU.mult))
            eng.wait_ge(S("lam_e"), 1)
            ch.link(v.tensor_tensor(la_[:, 4:5], la_[:, 3:4], la_[:, 2:3], ALU.subtract))
            v.tensor_scalar(la_[:, 4:5], la_[:, 4:5], -LAM_INIT, None, ALU.add).then_inc(S("cn"), 1)
            eng.wait_ge(S("cn"), 1)
            NL = la_[:, 4:5]
            for h in range(HC + 1):
                if h < HC:
                    q = h % 2
                    eng.wait_ge(S("s_qk"), h + 1)
                    ch.add(v.tensor_reduce(la_[:, 8 + 8 * q:10 + 8 * q], PS[:, 2 * q:2 * q + 2, 0:128], AX.X, ALU.max,
                                           negate=True))
                    v.tensor_reduce(la_[:, 10 + 8 * q:12 + 8 * q], PS[:, 2 * q:2 * q + 2, 128:384], AX.X, ALU.max,
                                    negate=True).then_inc(S("smax"), 1)
                if h >= 1:
                    q = (h - 1) % 2
                    L = la_[:, 24 + 8 * q:28 + 8 * q]
                    eng.wait_ge(S("sexp"), 4 * h)
                    ch.link(v.reciprocal(L, L))
                    L2v = L.rearrange("p (t c) -> p t c", c=2)
                    ch.add(v.tensor_scalar(L2v[:, :, 1:2], L2v[:, :, 1:2], NL, None, ALU.mult))
                    for t in range(2):
                        w0, w1 = ((0, 128), (128, 384))[t]
                        ch.add(v.tensor_scalar(PC[:, q, w0:w1], PP[:, q, w0:w1], L[:, 2 * t:2 * t + 1], None, ALU.mult))
                    ch.settle()
                    for t in range(2):
                        w0, w1 = ((0, 128), (128, 384))[t]
                        v.scalar_tensor_tensor(out=PC[:, q, w0:w1], in0=PP[:, q, 384 + w0:384 + w1],
                                               scalar=L[:, 2 * t + 1:2 * t + 2], in1=PC[:, q, w0:w1],
                                               op0=ALU.mult, op1=ALU.add).then_inc(S("pc"), 1)
                if h in (5, 8):
                    h4 = 0 if h == 5 else 4
                    eng.wait_ge(S("pv"), 4 + h4)
                    for t in range(2):
                        r = v.tensor_copy(OS[:, 8 * t + h4:8 * t + h4 + 4, :],
                                          PS[:, 6 + t, :].rearrange("p (a b) -> p a b", b=128))
                        r.then_inc(S("os"), 1)
            for gq in range(2):
                eng.wait_ge(S("s_qks"), gq + 1)
                v.tensor_reduce(la_[:, 40:42], PS[:, 0:4, :].rearrange("p (c a) b -> p c (a b)", c=2)[:, :, 0:544],
                                AX.X, ALU.max, negate=True).then_inc(S("ssmax"), 1)
                L = la_[:, 44:46]
                eng.wait_ge(S("ssexp"), 2 * gq + 2)
                ch.link(v.reciprocal(L, L))
                ch.add(v.tensor_scalar(L[:, 1:2], L[:, 1:2], NL, None, ALU.mult))
                ch.link(v.tensor_scalar(PCs[:, 0, :], PPs[:, 0, :], L[:, 0:1], None, ALU.mult))
                v.scalar_tensor_tensor(out=PCs[:, 0, :], in0=PPs[:, 1, :], scalar=L[:, 1:2], in1=PCs[:, 0, :],
                                       op0=ALU.mult, op1=ALU.add).then_inc(S("pcs"), 1)
                eng.wait_ge(S("pvs"), gq + 1)
                v.tensor_copy(OS[:, 16 + gq, :], PS[:, 6, 0:128]).then_inc(S("os"), 1)
            eng.wait_ge(S("os"), 6)
            sqv = QZ.rearrange("p a b -> p (a b)")[:, 0:18 * 128].rearrange("p (a b) -> p a b", b=128)
            ch.link(v.tensor_tensor(sqv, OS, OS, ALU.mult))
            v.tensor_reduce(ss[:, :], sqv, AX.X, ALU.add).then_inc(S("os_ss"), 1)
            eng.wait_ge(S("os_rs"), 1)
            v.tensor_tensor(OS, OS, rstd[:, :].unsqueeze(2).to_broadcast([128, 18, 128]), ALU.mult)\
                .then_inc(S("os_n"), 1)
            residual(1)
            norm(3)
            peer(1)
            norm(4, last=True)

        @block.tensor
        def _(eng):
            t_ = nc.tensor
            mm = t_.matmul

            def transposes(n):
                for i, t in enumerate(TILES[n]):
                    eng.wait_ge(S("Hn"), 3 * n + i + 1)
                    for k in range(KT):
                        r = t_.transpose(PS[:, 2 * t + k // 4, 128 * (k % 4):128 * (k % 4) + 128],
                                         Hn[:, t, 128 * k:128 * k + 128], ident[:, :])
                    r.then_inc(S("tr"), 1)
                eng.wait_ge(S("hT_a"), 3 * (n + 1))
                eng.wait_ge(S("hT_v"), 3 * (n + 1))

            def landed(bb):
                eng.wait_ge(S(f"w_in{bb % WSLOTS}"), 16 * (bb // WSLOTS + 1))

            def block_fm(bb, bank):
                landed(bb)
                for k in range(KT):
                    r = mm(PS[:, bank, 0:NT], blkw(bb % WSLOTS, k), hT[:, k, 0:NT], start=(k == 0), stop=(k == KT - 1))
                r.then_inc(S("blk"), 1)

            eng.wait_ge(S("consts"), 1)
            transposes(0)
            for t in range(3):
                for k in range(KT):
                    r = mm(PS[:, 4, 8 * t:8 * t + 8], hT[:, k, 128 * t:128 * t + 128], WBA[:, k, :],
                           start=(k == 0), stop=(k == KT - 1))
            r.then_inc(S("ba_mm"), 1)
            for bb in range(24):
                if bb >= 4:
                    eng.wait_ge(S("ev0"), bb - 3)
                block_fm(bb, bb % 4)
                if bb in (15, 16):
                    for i in range(4 * (bb - 15), 4 * (bb - 15) + 4):
                        eng.wait_ge(S("qk_sq"), i + 1)
                        if i >= 4:
                            eng.wait_ge(S("l2_sqrt"), i - 3)
                        else:
                            eng.wait_ge(S("ba"), 1)
                        mm(PS[:, 4 + i % 4, 0:291], ones[:, :], RN[:, i, :], start=True, stop=True)\
                            .then_inc(S("l2"), 1)
            eng.wait_ge(S("l2_sqrt"), 8)
            eng.wait_ge(S("conv"), 16)
            for i in range(8):
                if i >= 2:
                    eng.wait_ge(S("gate_th"), i - 1)
                mm(PS[:, 4 + i % 2, 0:291], GW[:, i // 4, i % 4, :], CV[:, 12 + i % 4, :], start=True, stop=True)\
                    .then_inc(S("gmm"), 1)
            eng.wait_ge(S("softplus"), 1)
            eng.wait_ge(S("gate_th"), 8)
            eng.wait_ge(S("ev0"), 24)
            mm(PS[:, 7, 0:8], LTp, G9[:, 0:8], start=True, stop=True)
            mm(PS[:, 7, 8:9], LTs, G9[:, 8:9], start=True, stop=True).then_inc(S("gc_mm"), 1)
            eng.wait_ge(S("qu"), 8)
            for bt, (u0, u1) in enumerate(BT):
                b0 = (0, 3, 6)[bt]
                for u in range(u0, u1):
                    c = 128 * (u - u0)
                    r = mm(PS[:, b0, c:c + 128], G9[:, u:u + 1].to_broadcast([128, 128]), LTp if bt < 2 else LTs,
                           start=True, stop=True)
                if bt < 2:
                    r.then_inc(S("gcB"), 1)
                for u in range(u0, u1):
                    c = 128 * (u - u0)
                    o = PS[:, b0 + 1, c:c + 128] if bt < 2 else PS[:, 6, 128:256]
                    mm(o, KU[:, u, :], KU[:, u, :], start=True, stop=True)
                for u in range(u0, u1):
                    c = 128 * (u - u0)
                    o = PS[:, b0 + 2, c:c + 128] if bt < 2 else PS[:, 6, 256:384]
                    r = mm(o, KU[:, u, :], QU[:, u, :], start=True, stop=True)
                r.then_inc(S("kk"), 1)
            for bt, (u0, u1) in enumerate(BT):
                eng.wait_ge(S("A"), u1)
                if bt == 2:
                    eng.wait_ge(S("gc"), 1)
                for u in range(u0, u1):
                    c = 128 * (u - u0)
                    r = t_.transpose(PS[:, (1, 4, 7)[bt], c:c + 128], Am[:, u, :], ident[:, :])
                r.then_inc(S("at_mm"), 1)
            eng.wait_ge(S("silu"), 12)
            for bt, (u0, u1) in enumerate(BT):
                eng.wait_ge(S("aq"), bt + 1)
                eng.wait_ge(S("expE"), bt + 1)
                eng.wait_ge(S("tds"), bt + 1)
                kb, vb = ((0, 2), (3, 5), (6, 6))[bt]
                for u in range(u0, u1):
                    c = 128 * (u - u0)
                    cv = c if bt < 2 else 128
                    t_.transpose(PS[:, kb, c:c + 128], KU[:, u, :], ident[:, :])
                    r = t_.transpose(PS[:, vb, cv:cv + 128], VU[:, u, :], ident[:, :])
                r.then_inc(S("kv_tr"), 1)
            for st, name in enumerate(INV):
                for bt, (u0, u1) in enumerate(BT):
                    bk = (0, 4, 0)[bt]
                    if st == 0:
                        eng.wait_ge(S("t0"), bt + 1)
                        eng.wait_ge(S("kbe"), 9)
                        eng.wait_ge(S("at"), 3)
                        eng.wait_ge(S("bmT"), 3)
                    else:
                        eng.wait_ge(S("inv_a"), inv_count(INV_A, st - 1, bt))
                        eng.wait_ge(S("inv_v"), inv_count(INV_V, st - 1, bt))
                    if bt == 0 and st:
                        eng.wait_ge(S("inv_a"), inv_count(INV_A, st - 1, 2))
                        eng.wait_ge(S("inv_v"), inv_count(INV_V, st - 1, 2))
                    if bt == 2:
                        if INV_A[name]:
                            eng.wait_ge(S("inv_a"), inv_count(INV_A, st, 0))
                        if INV_V[name]:
                            eng.wait_ge(S("inv_v"), inv_count(INV_V, st, 0))
                    prods = {
                        "a2": ((P1T, P1), (P1, P1T)),
                        "n2": ((P2T, Tm), (Tm, P2T), (P2T, P2), (P2, P2T)),
                        "n4": ((P4T, Tm), (Tm, P4T), (P4, P4T)),
                        "n8": ((P8T, Tm), (Tm, P8T)),
                        "x1": ((B1T, Tm),), "x2": ((B2T, Tm),), "x3": ((B3T, Tm),),
                        "m1": ((TTm, XM), (XM, TTm)), "m2": ((TTm, XM), (XM, TTm)), "m3": (None, (XM, TTm)),
                    }[name]
                    for i, pr in enumerate(prods):
                        if pr is None:
                            continue
                        for u in range(u0, u1):
                            c = 128 * (u - u0)
                            r = mm(PS[:, bk + i, c:c + 128], pr[0][:, u, :], pr[1][:, u, :], start=True, stop=True)
                    r.then_inc(S("inv_mm"), 1)
            eng.wait_ge(S("inv_v"), inv_count(INV_V, len(INV) - 1, 2))
            for bt, (u0, u1) in enumerate(BT):
                for u in range(u0, u1):
                    c = 128 * (u - u0)
                    r = mm(PS[:, (0, 4, 1)[bt], c:c + 128], KBE[:, u, :], TTm[:, u, :], start=True, stop=True)
                r.then_inc(S("w_mm"), 1)
            for u in range(4):
                r = mm(PS[:, 2, 128 * u:128 * u + 128], TTm[:, u, :], BV[:, u, :], start=True, stop=True)
            r.then_inc(S("vn_mm"), 1)
            eng.wait_ge(S("nw"), 3)
            mm(PS[:, 3, 0:128], TTm[:, 8, :], BV[:, 8, :], start=True, stop=False, skip_group_check=True)
            for h in range(4):
                r = mm(PS[32 * h:32 * h + 32, 3, 0:128], NW[:, 8, 32 * h:32 * h + 32], S0[:, h, :], start=False,
                       stop=(h == 3), skip_group_check=True)
            r.then_inc(S("vn_mm"), 1)
            eng.wait_ge(S("vn"), 1)
            eng.wait_ge(S("qe"), 3)
            for u in range(4):
                r = mm(PS[:, 6, 128 * u:128 * u + 128], DT[:, u, :], VN[:, u, :], start=True, stop=True)
            r.then_inc(S("o_mm"), 1)
            for u in range(4):
                r = mm(PS[:, 4, 128 * u:128 * u + 128], KDEC[:, u, :], VN[:, u, :], start=True, stop=True)
            r.then_inc(S("s_mm"), 1)
            eng.wait_ge(S("vn"), 2)
            mm(PS[:, 7, 0:128], DT[:, 8, :], VN[:, 8, :], start=True, stop=False, skip_group_check=True)
            for h in range(4):
                r = mm(PS[32 * h:32 * h + 32, 7, 0:128], E[:, 8, 32 * h:32 * h + 32], S0[:, h, :], start=False,
                       stop=(h == 3), skip_group_check=True)
            r.then_inc(S("o_mm"), 1)
            mm(PS[:, 0, :], KDEC[:, 8, :], VNm.rearrange("p a b -> p (a b)"), start=True, stop=True)\
                .then_inc(S("s_mm"), 1)
            eng.wait_ge(S("s1"), 1)
            for h in range(4):
                o = PS[:, 5, 128 * h:128 * h + 128]
                mm(o, TTm[:, 4 + h, :], BV[:, 4 + h, :], start=True, stop=False)
                r = mm(o, NW[:, 4 + h, :], S1[:, h, :], start=False, stop=True)
            r.then_inc(S("vn_mm"), 1)
            eng.wait_ge(S("vn"), 3)
            for h in range(4):
                o = PS[:, 1, 128 * h:128 * h + 128]
                mm(o, E[:, 4 + h, :], S1[:, h, :], start=True, stop=False)
                r = mm(o, DT[:, 4 + h, :], VN[:, 4 + h, :], start=False, stop=True)
            r.then_inc(S("o_mm"), 1)
            for h in range(4):
                r = mm(PS[:, 4, 128 * h:128 * h + 128], KDEC[:, 4 + h, :], VN[:, 4 + h, :], start=True, stop=True)
            r.then_inc(S("s_mm"), 1)
            for bt, (u0, u1) in enumerate(BT):
                eng.wait_ge(S("on"), bt + 1)
                for u in range(u0, u1):
                    c = 128 * (u - u0)
                    r = t_.transpose(PS[:, (2, 3, 5)[bt], c:c + 128], ON[:, u, :], ident[:, :])
                r.then_inc(S("on_tr"), 1)

            def out_proj(l):
                for j in range(8):
                    bb = (B_OUT0, B_OUT1)[l] + j
                    landed(bb)
                    for t in range(3):
                        for k in range(KT):
                            r = mm(PS[:, 2 * t + j // 4, 128 * (j % 4):128 * (j % 4) + 128],
                                   mixT[:, k, 128 * t:128 * t + 128], blkw(bb % WSLOTS, k),
                                   start=(k == 0), stop=(k == KT - 1))
                    r.then_inc(S("blk"), 1)

            eng.wait_ge(S("mix_d"), 1)
            eng.wait_ge(S("mix_lru"), 1)
            eng.wait_ge(S("sfin"), 2)
            out_proj(0)
            transposes(1)

            def peer(l):
                bq = (B_Q0, B_Q1)[l]

                def score(j):
                    eng.wait_ge(S("qt"), 16 * l + j + 1)
                    if j >= 4:
                        eng.wait_ge(S("sc"), 16 * l + j - 3)
                    q = 32 * ((j // 2) % 4)
                    kt = keysT[:, l, j % 2, :]
                    for t in range(2):
                        mm(PS[:, j % 4, 128 * t:128 * t + 128], QT[:, j % 4, 128 * t:128 * t + 128], kt,
                           start=True, stop=True)
                    mm(PS[q:q + 32, j % 4, 256:384], QT[:, j % 4, NP:NT], kt, start=True, stop=True)\
                        .then_inc(S("sc_mm"), 1)
                for j in range(16):
                    if j >= 2:
                        eng.wait_ge(S("qt"), 16 * l + j - 1)
                    block_fm(bq + j, 4 + j % 2)
                    if j >= 1:
                        score(j - 1)
                score(15)
                eng.wait_ge(S("sc"), 16 * l + 16)
                base = 288 * l
                for un, n in enumerate((2, 8, 8)):
                    a0 = (0, 4, 6)[un]
                    for half in range(2):
                        mm(PS[:, a0 + half, :], ZR[:, 0:128], ZR[:, :], start=True, stop=False, skip_group_check=True)
                    with eng.Fori(0, n) as i:
                        for c in range(16):
                            sl = c % UVS
                            eng.wait_ge(S("diag"), i * 16 + (base + c + 1))
                            mm(PS[:, a0, :], DG[:, sl, :], UV[:, sl, D:D + 512], start=False, stop=False,
                               skip_group_check=True)
                            mm(PS[:, a0 + 1, :], DG[:, sl, :], UV[:, sl, D + 512:2 * D], start=False, stop=False,
                               skip_group_check=True).then_inc(S(f"uv_free{sl}"), 1)
                    base += 16 * n
                    for half in range(2):
                        r = mm(PS[:, a0 + half, :], ZR[:, 0:128], ZR[:, :], start=False, stop=True,
                               skip_group_check=True)
                    r.then_inc(S("acc"), 1)
                    if un == 0:
                        for half in range(2):
                            eng.wait_ge(S("ys"), 4 * l // 2 + half + 1)
                            r = mm(PS[:, 2 + half, :], RP[:, :],
                                   YS[:, 512 * half:512 * half + 512],
                                   start=True, stop=True)
                        r.then_inc(S("acc"), 1)

            peer(0)
            transposes(2)
            for j in range(24):
                if j >= 4:
                    eng.wait_ge(S("ev1"), j - 3)
                if j < 16:
                    block_fm(B_QKV + j, j % 4)
                else:
                    bb = B_QKV + j
                    landed(bb)
                    for t in range(3):
                        for k in range(KT):
                            r = mm(PS[:, j % 4, 128 * t:128 * t + 128], hT[:, k, 128 * t:128 * t + 128],
                                   blkw(bb % WSLOTS, k), start=(k == 0), stop=(k == KT - 1))
                    r.then_inc(S("blk"), 1)
            eng.wait_ge(S("ev1"), 24)

            def qk(h):
                if h >= 2:
                    eng.wait_ge(S("sexp"), 4 * (h - 1))
                for c in range(2):
                    bank = PS[:, 2 * (h % 2) + c, :]
                    mm(bank[:, 0:384], ident[:, :], msk, start=True, stop=False)
                    mm(bank[:, 0:128], QZ[:, 2 * h + c, 0:128], KTt[:, h, 0:128], start=False, stop=False)
                    r = mm(bank[:, 128:384], QZ[:, 2 * h + c, 128:256], KTt[:, h, 0:256], start=False, stop=True)
                r.then_inc(S("s_qk"), 1)

            def p_transposes(h):
                eng.wait_ge(S("pc"), 2 * h + 2)
                for i in range(3):
                    r = t_.transpose(PS[:, 4 + h % 2, 128 * i:128 * i + 128], PC[:, h % 2, 128 * i:128 * i + 128],
                                     ident[:, :])
                r.then_inc(S("p_tr"), 1)

            def pv(h):
                eng.wait_ge(S("pt"), h + 1)
                if h == 4:
                    eng.wait_ge(S("os"), 2)
                c = 128 * (h % 4)
                pt = PTt[:, h % 2, :]
                vh = lambda t: Vt[:, t, 128 * h:128 * h + 128]
                mm(PS[:, 6, c:c + 128], pt[:, 0:128], vh(0), start=True, stop=True)
                mm(PS[:, 7, c:c + 128], pt[:, 128:256], vh(0), start=True, stop=False)
                mm(PS[:, 7, c:c + 128], pt[:, 256:384], vh(1), start=False, stop=True).then_inc(S("pv"), 1)

            for h in range(HC + 2):
                if h < HC:
                    qk(h)
                if 1 <= h <= HC:
                    p_transposes(h - 1)
                if h >= 2:
                    pv(h - 2)
            eng.wait_ge(S("kc"), 16)
            eng.wait_ge(S("vc"), 16)
            eng.wait_ge(S("sexp"), 4 * HC)
            eng.wait_ge(S("os"), 4)
            for gq in range(2):
                if gq:
                    eng.wait_ge(S("ssexp"), 2)
                for c in range(2):
                    for j in range(4):
                        h = 4 * gq + j
                        qz = QZ[:, 2 * h + c, NP:NT]
                        mm(PS[32 * j:32 * j + 32, 2 * c, :], qz, KC[:, h, :], start=True, stop=True)
                        r = mm(PS[32 * j:32 * j + 32, 2 * c + 1, 0:32], qz, KTt[:, h, NP:NT], start=True, stop=True)
                r.then_inc(S("s_qks"), 1)
                eng.wait_ge(S("pcs"), gq + 1)
                for i in range(4):
                    t_.transpose(PS[:, 4, 128 * i:128 * i + 128], PCs[:, 0, 128 * i:128 * i + 128], ident[:, :])
                t_.transpose(PS[0:32, 5, 0:128], PCs[:, 0, 512:544], ident[:, :]).then_inc(S("ps_tr"), 1)
                eng.wait_ge(S("pts"), gq + 1)
                if gq:
                    eng.wait_ge(S("os"), 5)
                ptf = PTt.rearrange("p a b -> p (a b)")
                for j in range(4):
                    h = 4 * gq + j
                    o = PS[32 * j:32 * j + 32, 6, 0:128]
                    for i in range(4):
                        mm(o, ptf[:, 128 * i + 32 * j:128 * i + 32 * j + 32], VC[:, i, 128 * h:128 * h + 128],
                           start=(i == 0), stop=False)
                    r = mm(o, ptf[0:32, 512 + 32 * j:512 + 32 * j + 32], Vt[0:32, 2, 128 * h:128 * h + 128],
                           start=False, stop=True)
                r.then_inc(S("pvs"), 1)
            eng.wait_ge(S("os_n"), 1)
            for i in range(5):
                for u in range(4 * i, min(4 * i + 4, 18)):
                    c = 128 * (u - 4 * i)
                    r = t_.transpose(PS[:, i, c:c + 128], OS[:, u, :], ident[:, :])
                r.then_inc(S("o_tr"), 1)
            eng.wait_ge(S("mix1"), 12)
            out_proj(1)
            transposes(3)
            peer(1)


def layout(inputs):
    import numpy as np
    f = {k: np.asarray(v) for k, v in inputs.items()}
    tile = lambda v, n: np.concatenate([v] * n, axis=0)
    pcol = lambda v: np.ascontiguousarray(v.reshape(-1, 128).T)
    xs = f["x_sample"][0]
    x = np.stack([f["x_prompt"][0, 0:128], f["x_prompt"][0, 128:256], tile(xs, 4)], axis=1)
    blk = lambda w: np.ascontiguousarray(w.reshape(8, 128, -1, 128).transpose(2, 1, 0, 3)).reshape(-1, 128, 1024)
    wi = f["ab_w_in"][0]
    w = np.concatenate([blk(wi[:, 0:2048]), blk(wi[:, 2056:3080]), blk(f["ab_w_out"][0]), blk(f["peer_w_query"][0]),
                        blk(f["c_w_qkv"][0]), blk(f["c_w_out"][0]), blk(f["peer_w_query"][1])])
    assert w.shape[0] == NBLK
    wba = np.ascontiguousarray(wi[:, 2048:2056].reshape(8, 128, 8).transpose(1, 0, 2)).reshape(128, 64)
    cw = np.concatenate([f["a_conv_w"][0], f["b_conv_w"][0]], axis=1)
    cw = cw.reshape(4, 16, 128).transpose(2, 1, 0).reshape(128, 64)
    heads = lambda v: np.concatenate([np.broadcast_to(v[None, :], (128, 4))] * 2 + [np.repeat(v, 32)[:, None]], axis=1)
    cols = np.concatenate([
        cw, pcol(f["b_conv_b"][0]), heads(f["a_log"][0]), heads(f["a_dt_bias"][0]), pcol(f["b_lambda"][0]),
        pcol(f["b_gate_a_b"][0]), pcol(f["b_gate_x_b"][0]), f["a_norm"][0][:, None], f["c_norm"][0][:, None],
        pcol(f["state_b_rglru"][0, 0])], axis=1)
    assert cols.shape == (128, NCOL)
    st = np.concatenate([f["state_a_conv"][0, 0], f["state_b_conv"][0, 0]], axis=1)
    st = st.reshape(3, 16, 128).transpose(2, 1, 0).reshape(128, 48)
    gw = np.zeros((128, 2, 4, 128), np.float32)
    for i, n in enumerate(("b_gate_a_w", "b_gate_x_w")):
        for q in range(8):
            o = 64 * (q % 2)
            gw[o:o + 64, i, q // 2, o:o + 64] = f[n][0, q]
    c = np.ascontiguousarray
    return {
        "x": c(x), "w": w, "wba": wba, "cols": c(cols), "st_conv": c(st), "gw": gw.reshape(128, 1024),
        "gains": np.stack([f["norm_mix"][0], f["norm_ffn"][0], f["norm_mix"][1], f["norm_ffn"][1], f["norm_final"]]),
        "s0": c(f["state_a_delta"][0, 0].transpose(1, 0, 2)).reshape(128, 512),
        "keys": c(f["peer_sub_keys"].transpose(3, 0, 1, 2)).reshape(128, 512),
        "uv0": np.concatenate([f["peer_u"][0], f["peer_v"][0]], axis=1),
        "uv1": np.concatenate([f["peer_u"][1], f["peer_v"][1]], axis=1),
        "lq": np.stack([f["c_lambda_q1"][0], f["c_lambda_q2"][0], f["c_lambda_k1"][0], f["c_lambda_k2"][0]])
        .reshape(1, 256),
        "kc": c(f["cache_c_k"][0, 0].reshape(512, 8, 128).transpose(2, 1, 0)).reshape(128, 4096),
        "vc": c(f["cache_c_v"][0, 0].reshape(4, 128, 1024).transpose(1, 0, 2)).reshape(128, 4096),
    }


OUTS = {"o_y": (128, 3, 1024), "o_conv": (128, 96), "o_dp": (128, 512), "o_ds": (128, 512), "o_h": (128, 8),
        "o_k": (128, 8 * 288), "o_v": (128, 3 * 1024)}


def kernel(**inputs):
    import numpy as np
    import concourse.bacc as bacc
    from concourse import mybir
    from concourse.bass_utils import run_bass_kernel_spmd as run

    nc = bacc.Bacc("TRN2", target_bir_lowering=False, num_devices=1)
    arrays = layout(inputs)
    outs = dict(OUTS)
    DBG = False
    if DBG:
        outs["dbg"] = (128, 3, 1024)
    F = mybir.dt.float32
    T = {k: nc.dram_tensor("in_" + k, v.shape, F, kind="ExternalInput").ap() for k, v in arrays.items()}
    T.update({k: nc.dram_tensor("out_" + k, s, F, kind="ExternalOutput").ap() for k, s in outs.items()})
    build(nc, T, DBG)
    r = run(nc, [{"in_" + k: v for k, v in arrays.items()}], core_ids=[0]).results[0]
    r = {k: r["out_" + k] for k in outs}
    y = r["o_y"].reshape(128, 3, 1024)
    yp = np.concatenate([y[:, 0], y[:, 1]])[None]
    ys = y[0:32, 2][None]
    cs = r["o_conv"].reshape(128, 16, 2, 3).transpose(2, 3, 1, 0).reshape(2, 3, 2048)
    ds = [r[n].reshape(128, 4, 128).transpose(1, 0, 2)[None, None] for n in ("o_dp", "o_ds")]
    hs = r["o_h"].reshape(128, 4, 2).transpose(2, 1, 0).reshape(2, 512)
    k = r["o_k"].reshape(128, 8, 288).transpose(2, 1, 0)
    v = r["o_v"].reshape(128, 3, 1024)
    vp = np.concatenate([v[:, 0], v[:, 1]])
    return (yp, ys, cs[0, :, 0:1536][None, None], ds[0], cs[0, :, 1536:][None, None], hs[0][None, None],
            k[0:256].reshape(1, 1, 256, 8, 2, 64), vp.reshape(1, 1, 256, 8, 128),
            cs[1, :, 0:1536][None, None], ds[1], cs[1, :, 1536:][None, None], hs[1][None, None],
            k[256:].reshape(1, 1, 32, 8, 2, 64), v[0:32, 2].reshape(1, 1, 32, 8, 128))
```

```python
import math
from contextlib import ExitStack

D = 1024
KT = D // 128
NP = 256
NS = 32
NT = NP + NS
H = 4
HC = 8
PAST = 512
EPS = 1e-6
TOPK = 16
NKEY = 128
PH = 8
WSLOTS = 4
UVS = 8
NEG = -1e30
B_IN, B_OUT0, B_Q0 = 0, 24, 32
B_QKV, B_OUT1, B_Q1 = 48, 72, 80
NBLK = 96
ARENA = 30770
C_CW, C_CB, C_AL, C_DT, C_LM, C_GA, C_GX, C_AN, C_CN, C_H0, NCOL = 0, 64, 68, 77, 86, 90, 94, 98, 99, 100, 104
NORMS = ((0, (0, 1, 2)), (1, (0, 1, 2)), (2, (2, 0)), (3, (2, 0)), (2, (1,)), (3, (1,)), (4, (2, 0)), (4, (1,)))
NORM_AT = [sum(len(t) for _, t in NORMS[:k]) for k in range(len(NORMS) + 1)]
GAIN_LOAD = (0, 1, 2, 3, 4, 5, 6, 6)
UNITS = ((256, 2, 0, 32), (0, 0, 32, 128), (128, 1, 160, 128), (256, 2, 288, 32), (0, 0, 320, 128), (128, 1, 448, 128))
ACC = (2, 3, 4, 6, 7, 8)


AHEAD = 296
PE_LAG = 2
PACE = ((2, 1, 2, 5, 2, 2.5), (2, 2, 3, 0, 2, 2))


def step_plan():
    plan = {}
    for ps, m, misc, qkv, head, smp, out, q in ((0, 160) + PACE[0], (1, AHEAD) + PACE[1]):
        for kind, n, k in (("norm2", 1, misc), ("qkv", 24, qkv), ("head", 10, head), ("smp", 4 * (1 - ps), smp),
                           ("on", 1, misc), ("out", 8, out), ("norm3", 1, misc), ("q", 18 - 2 * ps, q)):
            for j in range(n):
                m += k
                plan[ps, kind, j] = int(m)
    assert plan[0, "q", 15] < 288 and plan[0, "q", 17] <= AHEAD and plan[1, "q", 15] <= 448
    return plan


PLAN = step_plan()
LAM_INIT = 0.8 - 0.6 * math.exp(-0.3)


def build(nc, T):
    import concourse.bass as bass
    from concourse import mybir

    F, U = mybir.dt.float32, mybir.dt.uint32
    ALU, ACT, AX = mybir.AluOpType, mybir.ActivationFunctionType, mybir.AxisListType

    with ExitStack() as ctx:
        def sb(name, shape, dt=F):
            return ctx.enter_context(nc.sbuf_tensor("sb_" + name, shape, dt))

        sems = {}

        def S(name):
            if name not in sems:
                sems[name] = ctx.enter_context(nc.semaphore(name))
            return sems[name]

        class Chain:

            def __init__(self, eng, name):
                self.eng, self.name = eng, name
                self.sem, self.n, self.looping = S(name), 0, False

            def add(self, ins):
                self.n += 1
                ins.then_inc(self.sem, 1)

            def settle(self):
                if self.looping and self.n == 0:
                    return
                self.eng.wait_ge(self.sem, self.n)
                if self.looping:
                    self.eng.sem_clear(self.sem)
                    self.n = 0

            def link(self, ins):
                self.add(ins)
                self.settle()

            def loop(self):
                self.settle()
                self.kept, self.sem, self.n, self.looping = self.n, S(self.name + "_loop"), 0, True

            def loop_end(self):
                assert self.n == 0
                self.sem, self.n, self.looping = S(self.name), self.kept, False

        X = sb("X", [128, 3, D])
        Hn = sb("Hn", [128, 3, D])
        hT = sb("hT", [128, KT, 384])
        W = sb("W", [128, WSLOTS, KT * 128])
        gB = sb("gB", [128, D])
        cols = sb("cols", [128, NCOL])
        keysT = sb("keysT", [128, 2, 2, NKEY])
        ident = sb("ident", [128, 128])
        ones = sb("ones", [128, 128])
        bm16 = sb("bm16", [128, 128])
        bm32 = sb("bm32", [128, 128])
        bm64 = sb("bm64", [128, 128])
        mhalf = sb("mhalf", [128, 18])
        ss = sb("ss", [128, 18])
        rstd = sb("rstd", [128, 18])
        mixT = sb("mixT", [128, 8, 384])
        AR = sb("AR", [128, ARENA])
        PS = ctx.enter_context(nc.psum_tensor("PS", [128, 8, 512], F))

        class Arena:
            def __init__(self, at=0):
                self.at = at

            def __call__(self, *shape, dt=F):
                n = 1
                for s in shape:
                    n *= s
                v = AR[:, self.at:self.at + n]
                self.at += n
                assert self.at <= ARENA, self.at
                if dt is not F:
                    v = v.bitcast(dt)
                if len(shape) == 2:
                    return v.rearrange("p (a b) -> p a b", b=shape[1])
                if len(shape) == 3:
                    return v.rearrange("p (a b c) -> p a b c", b=shape[1], c=shape[2])
                return v

        a = Arena()
        PJ = a(16, 294)
        CV = a(16, 291)
        QK = a(8, 291)
        RN = a(8, 291)
        QU, KU, VU = a(9, 128), a(9, 128), a(9, 128)
        Dm, DT, E = a(9, 128), a(9, 128), a(9, 128)
        KBE, KDEC, BV = a(9, 128), a(9, 128), a(9, 128)
        SZ = a(4, NT)
        GG = a(4, NT)
        S0, S1, S2 = a(4, 128), a(4, 128), a(4, 128)
        GW = a(2, 4, 128)
        sm = a(256)
        MDT, MDTs, MDs, MDss = a(128), a(128), a(128), a(128)
        LTp, LTs = a(128), a(128)
        CSi = a(16, 3)
        CSo = a(16, 6)
        WBA = a(8, 8)
        b = Arena(0)
        Am, AT_, P1, P1T = (b(9, 128) for _ in range(4))
        MX = mixT[:, :, :].rearrange("p a b -> p (a b)")
        TTm = MX[:, 0:1152].rearrange("p (a b) -> p a b", b=128)
        Tm = MX[:, 1536:2688].rearrange("p (a b) -> p a b", b=128)
        b = Arena(16 * 294)
        B1T, B2T, B3T = (b(9, 128) for _ in range(3))
        b = Arena(16 * 294 + 16 * 291)
        TD, TS, XM, NW = (b(9, 128) for _ in range(4))
        P2, P2T, P4, P4T, P8T = TD, TS, P1, P1T, TD
        VN = Dm
        VNm = TS[:, 0:4, :]
        ON = Am
        LR = Hn[:, :, :].rearrange("p a b -> p (a b)")
        L1 = LR[:, 0:4 * 291].rearrange("p (a b) -> p a b", b=291)
        L2 = LR[:, 4 * 291:8 * 291].rearrange("p (a b) -> p a b", b=291)
        HTf = hT[:, :, :].rearrange("p a b -> p (a b)")
        L3 = HTf[:, 0:4 * 291].rearrange("p (a b) -> p a b", b=291)
        L4 = HTf[:, 4 * 291:8 * 291].rearrange("p (a b) -> p a b", b=291)

        a = Arena()
        UV = a(UVS, 2 * D)
        QZ = a(8 * 2, 160)
        KTt = a(8, NT)
        Vt = a(3, D)
        shared = a.at
        SC0 = a(8, NKEY)
        SC1 = a(16, NKEY)
        SCS = a(4, NKEY)
        QT = a(4, NT)
        YS = QT.rearrange("p a b -> p (a b)")[:, 0:D]
        rows = a(2, NKEY)
        tm = a(2, NKEY)
        cand = a(16, 16)
        candt = a(16 * 16)
        hot = a(32, 16)
        pv_, pi = a(2, 16), a(2, 16, dt=U)
        tv, sel = a(16), a(16, dt=U)
        ab = a(32, dt=U)
        i12 = a(32)
        gsum = sb("gsum", [128, 8])[:, :]
        a = Arena(shared)
        KC = a(4, PAST)
        VC = a(4, 512)
        PP = a(2, 512)
        PPs = Arena(a.at - 1024)(2, 544)
        a(64)
        PC = a(2, 256)
        PCs = Arena(a.at - 512)(1, 544)
        a(32)
        PTt = a(2, 320)
        sqs = Arena(shared)(10, 128)
        lq = Arena(a.at - 640)(4, 64)
        la_ = sb("la", [128, 64])[:, :]
        msk = bm16[:, :]
        ssn = sb("ssn", [128, 3])
        rtn = sb("rtn", [128, 3])
        rsn = sb("rsn", [128, 3])
        nwt = sb("nwt", [128, 10])
        idx = sb("idx", [128, 288], U)
        idst = sb("idst", [128, 16], U)
        gate = sb("gate", [128, 288])
        iota16 = sb("iota16", [128, 16])
        dots = sb("dots", [128, 8])
        gl = sb("gl", [128, 8])
        gst = sb("gst", [128, 16])
        DG = sb("DG", [128, UVS, 128])
        ZR = sb("ZR", [128, 512])
        RP = sb("RP", [128, 128])
        BA = sm[:, 0:24]
        AL, TH, MN, EX, SR, SQ_, PL, SP = (sm[:, 24 + 13 * i:24 + 13 * (i + 1)] for i in range(8))
        BE, GC, NGC, EGC, BEG, DEC, EAL, G9 = (sm[:, 130 + 9 * i:139 + 9 * i] for i in range(8))
        EGL = sm[:, 204:213]
        CLM = sm[:, 214:218]
        HB = sm[:, 218:226]
        egls = sm[:, 226:230]
        hlast = sm[:, 232:240]

        def blkw(s, k):
            return W[:, s, 128 * k:128 * k + 128]

        BT = [(0, 4), (4, 8), (8, 9)]
        INV = ["a2", "n2", "n4", "n8", "x1", "m1", "x2", "m2", "x3", "m3"]
        INV_A = {"a2": 1, "n2": 1, "n4": 1, "n8": 0, "x1": 1, "m1": 0, "x2": 1, "m2": 0, "x3": 1, "m3": 0}
        INV_V = {"a2": 1, "n2": 1, "n4": 1, "n8": 1, "x1": 0, "m1": 1, "x2": 0, "m2": 1, "x3": 0, "m3": 1}

        def inv_count(has, st, bt):
            n = 0
            for i, name in enumerate(INV):
                for t in range(3):
                    n += has[name]
                    if i == st and t == bt:
                        return n

        HCOL = {0: 0, 2: 128, 1: 256}

        def at(i, value):
            return value if i is None else i * 16 + value

        class Steps:

            def __init__(self, eng, step, begin=lambda q: None, end=lambda q: None):
                self.eng, self.step, self.begin, self.end, self.m = eng, step, begin, end, 0

            def edge(self, which):
                for q, (_, _, first, n) in enumerate(UNITS):
                    if which == "begin" and self.m == first:
                        self.begin(q)
                    if which == "end" and self.m == first + n:
                        self.end(q)

            def upto(self, m1):
                while self.m < m1:
                    self.edge("begin")
                    self.step(self.m)
                    self.m += 1
                    self.edge("end")

            def loop(self, m0, n, first=None):
                assert m0 == self.m
                self.edge("begin")
                with self.eng.Fori(0, n) as i:
                    if first is not None:
                        first(i)
                    for c in range(16):
                        self.step(m0 + c, i)
                self.m += 16 * n
                self.edge("end")

        block = ctx.enter_context(nc.Block())

        @block.sync
        def _(eng):
            d = nc.sync.dma_start
            for t in range(3):
                d(X[:, t, :], T["x"][:, t, :]).then_inc(S(f"x_in{t}"), 16)
            d(gB[:, :], T["gains"][0:1, :].to_broadcast([128, D])).then_inc(S("gain"), 16)
            for s in range(WSLOTS):
                d(W[:, s, :], T["w"][s]).then_inc(S(f"w_in{s}"), 16)

            def stream(b0, b1):
                back = 48 if b0 >= NBLK else 0
                with eng.Fori(0, (b1 - b0) // WSLOTS) as i:
                    for s in range(WSLOTS):
                        eng.wait_ge(S("blk"), i * WSLOTS + (b0 + s + 1 - WSLOTS))
                        d(W[:, s, :], T["w"][bass.ds(i * WSLOTS + (b0 - back + s), 1), :, :]
                          .rearrange("a p n -> (a p) n")).then_inc(S(f"w_in{s}"), 16)

            stream(WSLOTS, B_OUT0)
            eng.wait_ge(S("cso"), 2)
            d(T["o_conv"], CSo.rearrange("p a b -> p (a b)")).then_inc(S("out"), 16)
            stream(B_OUT0, B_OUT0 + WSLOTS)
            eng.wait_ge(S("Hn"), 3)
            d(gB[:, :], T["gains"][1:2, :].to_broadcast([128, D])).then_inc(S("gain"), 16)
            eng.wait_ge(S("sfin"), 2)
            d(T["o_dp"], S2.rearrange("p a b -> p (a b)")).then_inc(S("out"), 16)
            d(T["o_ds"], S0.rearrange("p a b -> p (a b)")).then_inc(S("out"), 16)
            eng.wait_ge(S("h_last"), 1)
            d(T["o_h"], hlast).then_inc(S("out"), 16)
            stream(B_OUT0 + WSLOTS, B_Q0 + WSLOTS)
            stream(B_Q0 + WSLOTS, B_QKV + WSLOTS)

            def gain(k, after):
                eng.wait_ge(S("Hn"), after)
                d(gB[:, :], T["gains"][k:k + 1, :].to_broadcast([128, D])).then_inc(S("gain"), 16)

            def caches(gq):
                d(KC.rearrange("p a b -> p (a b)"), T["kc"][:, 2048 * gq:2048 * gq + 2048]).then_inc(S("kc"), 16)
                d(VC, T["vc"].rearrange("p (a b) -> p a b", b=D)[:, :, 512 * gq:512 * gq + 512])\
                    .then_inc(S("vc"), 16)

            gain(2, NORM_AT[2])
            eng.wait_ge(S("idx"), 18)
            eng.wait_ge(S("x_peer"), 2)
            d(lq.rearrange("p a b -> p (a b)"), T["lq"].to_broadcast([128, 256])).then_inc(S("lq"), 16)
            caches(0)
            gain(3, NORM_AT[3])
            stream(B_QKV + WSLOTS, B_OUT1 + WSLOTS)
            eng.wait_ge(S("s_qks"), 1)
            eng.wait_ge(S("pvs"), 1)
            caches(1)
            stream(B_OUT1 + WSLOTS, B_Q1 + WSLOTS)
            gain(2, NORM_AT[4])
            stream(B_Q1 + WSLOTS, NBLK)
            stream(NBLK, NBLK + WSLOTS)
            gain(3, NORM_AT[5])
            stream(NBLK + WSLOTS, NBLK + 24 + WSLOTS)
            eng.wait_ge(S("ev1"), 48)
            d(T["o_k"], KTt.rearrange("p a b -> p (a b)")).then_inc(S("out"), 16)
            d(T["o_v"], Vt.rearrange("p a b -> p (a b)")).then_inc(S("out"), 16)
            stream(NBLK + 24 + WSLOTS, NBLK + 32 + WSLOTS)
            gain(4, NORM_AT[6])
            stream(NBLK + 32 + WSLOTS, NBLK + 48)
            for i, t in enumerate((2, 0, 1)):
                eng.wait_ge(S("Hn"), NORM_AT[6] + i + 1)
                d(T["o_y"][:, t, :], Hn[:, t, :]).then_inc(S("out"), 16)
            eng.wait_ge(S("out"), 16 * 9)

        @block.gpsimd
        def _(eng):
            g = nc.gpsimd
            ch = Chain(eng, "pool_own")
            ch.link(g.memset(ident[:, :], 0.0))
            g.affine_select(out=ident[:, :], in_=ident[:, :], compare_op=ALU.not_equal, fill=1.0,
                            base=0, pattern=[[-1, 128]], channel_multiplier=1).then_inc(S("ident"), 1)
            for m, v in ((ones, 1.0), (bm16, 1.0), (bm32, 1.0), (bm64, 1.0), (mhalf, -0.5), (ZR, 0.0)):
                ch.add(g.memset(m[:, :], v))
            ch.add(g.memset(RP[:, :], 0.0))
            for v in (MDT, MDs, ):
                ch.add(g.memset(v, 0.0))
            ch.add(g.memset(LTp, 1.0))
            ch.add(g.memset(PJ[:, :, 0:3], 0.0))
            ch.add(g.iota(iota16[:, :], pattern=[[1, 16]], base=0, channel_multiplier=0,
                          allow_small_or_imprecise_dtypes=True))
            ch.settle()
            for r in range(-3, 4):
                ch.link(g.affine_select(out=RP[:, :], in_=RP[:, :], compare_op=ALU.not_equal, fill=1.0,
                                        base=32 * r, pattern=[[-1, 128]], channel_multiplier=1))
            for m, n in ((bm16, 16), (bm32, 32), (bm64, 64)):
                v = m[:, :].rearrange("p (a b) -> p a b", b=n)
                ch.link(g.affine_select(out=v, in_=v, compare_op=ALU.is_ge, fill=0.0, base=0,
                                        pattern=[[-n, 128 // n], [0, n]], channel_multiplier=1))
                ch.add(g.affine_select(out=v, in_=v, compare_op=ALU.is_ge, fill=0.0, base=n - 1,
                                       pattern=[[n, 128 // n], [0, n]], channel_multiplier=-1))
            ch.add(g.affine_select(out=LTp, in_=LTp, compare_op=ALU.is_ge, fill=0.0, base=0,
                                   pattern=[[1, 128]], channel_multiplier=-1))
            ch.add(g.affine_select(out=MDT, in_=MDT, compare_op=ALU.is_ge, fill=NEG, base=0,
                                   pattern=[[1, 128]], channel_multiplier=-1))
            ch.add(g.affine_select(out=MDs, in_=MDs, compare_op=ALU.is_ge, fill=NEG, base=-1,
                                   pattern=[[-1, 128]], channel_multiplier=1))
            ch.settle()
            ch.add(g.tensor_tensor(LTs, LTp, bm32[:, :], ALU.mult))
            for o, m in ((MDTs, MDT), (MDss, MDs)):
                o3, m3 = (v.rearrange("p (a b) -> p a b", b=32) for v in (o, m))
                ch.link(g.affine_select(out=o3, in_=m3, compare_op=ALU.is_ge, fill=NEG, base=0,
                                        pattern=[[-32, 4], [0, 32]], channel_multiplier=1))
                ch.link(g.affine_select(out=o3, in_=o3, compare_op=ALU.is_ge, fill=NEG, base=31,
                                        pattern=[[32, 4], [0, 32]], channel_multiplier=-1))
            ch.settle()
            eng.wait_ge(S("par"), 16 * 6)
            g.tensor_copy(PJ[:, :, 259:262], CSi).then_inc(S("consts"), 1)

            for i in range(8):
                eng.wait_ge(S("silu"), i + 1)
                g.tensor_tensor(RN[:, i, :], QK[:, i, :], QK[:, i, :], ALU.mult).then_inc(S("qk_sq"), 1)
            eng.wait_ge(S("conv"), 16)
            g.tensor_copy(CSo[:, :, 0:3], PJ[:, :, 256:259]).then_inc(S("cso"), 1)
            g.tensor_copy(CSo[:, :, 3:6], PJ[:, :, 291:294]).then_inc(S("cso"), 1)
            eng.wait_ge(S("softplus"), 1)
            for f in range(4):
                eng.wait_ge(S("gate_th"), f + 1)
                g.tensor_scalar(L1[:, f, :], L1[:, f, :], 1.0, CLM[:, f:f + 1], ALU.add, ALU.mult)\
                    .then_inc(S("log_a"), 1)
            eng.wait_ge(S("lru_t"), 1)
            g.tensor_scalar(L1, L4, -1.0, 1.0, ALU.mult, ALU.add).then_inc(S("lru_den"), 1)
            for bt, (u0, u1) in enumerate(BT):
                eng.wait_ge(S("expE"), bt + 1)
                eng.wait_ge(S("qu"), 8)
                eng.wait_ge(S("egl"), bt + 1)
                g.tensor_tensor(E[:, u0:u1, :], E[:, u0:u1, :], QU[:, u0:u1, :], ALU.mult).then_inc(S("qe"), 1)
            eng.wait_ge(S("l2_sqrt"), 8)
            eng.wait_ge(S("qu"), 8)
            for k, (m1, m0) in enumerate(((bm32, bm16), (bm64, bm32), (ones, bm64))):
                ch.add(g.tensor_tensor(XM[:, k, :], m1[:, :], m0[:, :], ALU.subtract))
            ch.settle()
            for bt, (u0, u1) in enumerate(BT):
                n = u1 - u0
                eng.wait_ge(S("at"), bt + 1)
                for k, o in enumerate((B1T, B2T, B3T)):
                    r = g.tensor_tensor(o[:, u0:u1, :], AT_[:, u0:u1, :],
                                        XM[:, k:k + 1, :].to_broadcast([128, n, 128]), ALU.mult)
                r.then_inc(S("bmT"), 1)
            eng.wait_ge(S("lru_rec"), 4)
            g.tensor_tensor(L4, L4, L1, ALU.mult).then_inc(S("lru_q"), 1)
            eng.wait_ge(S("gate_th"), 8)
            ch.link(g.tensor_scalar(L2, L2, 1.0, None, ALU.add, ALU.bypass))
            ch.link(g.tensor_tensor(L2, L2, CV[:, 12:16, :], ALU.mult))
            eng.wait_ge(S("lru_sq"), 1)
            g.tensor_tensor(L2, L2, L4, ALU.mult).then_inc(S("lru_u"), 1)
            for bt, (u0, u1) in enumerate(BT):
                eng.wait_ge(S("o_ss"), u1)
                ch.link(g.tensor_scalar(ss[:, u0:u1], ss[:, u0:u1], 1.0 / 128, EPS, ALU.mult, ALU.add))
                g.tensor_tensor(rstd[:, u0:u1], ss[:, u0:u1], mhalf[:, u0:u1], ALU.pow).then_inc(S("o_rs"), 1)
            eng.wait_ge(S("hs"), 1)
            hl = hlast.rearrange("p (a b) -> p a b", b=2)
            g.tensor_copy(hl[:, :, 0:1], L1[:, :, 255:256])
            g.tensor_copy(hl[:, :, 1:2], L1[:, :, 290:291]).then_inc(S("h_last"), 1)
            g.tensor_tensor(mixT[:, 4:8, 0:NP], L1[:, :, 0:NP], GG[:, :, 0:NP], ALU.mult)
            for j in range(4):
                r = g.tensor_tensor(mixT[:, 4:8, NP + 32 * j:NP + 32 * j + 32], L1[:, :, 259:291],
                                    GG[:, :, NP:NT], ALU.mult)
            r.then_inc(S("mix_lru"), 1)

            def gather(l, cols_, half, refill):
                g.tensor_copy(idst[:, 8 * half:8 * half + 8], cols_).then_inc(S("staged"), 1)
                eng.wait_ge(S("staged"), 1)
                eng.sem_clear(S("staged"))
                for s in range(UVS):
                    if refill:
                        eng.wait_ge(S(f"uv_free{s}"), 1)
                        eng.sem_clear(S(f"uv_free{s}"))
                    g.indirect_dma_start(UV[:, s, :], None, T[f"uv{l}"], bass.IndirectOffsetOnAxis(
                        ap=idst[:, 8 * half + s:8 * half + s + 1], axis=0)).then_inc(S(f"uv_in{s}"), 16)

            for q, (c0, t, m0, n) in enumerate(UNITS):
                l = q // 3
                if n == 32:
                    for gq in range(2):
                        eng.wait_ge(S("idx"), 18 * l + 5 + 3 * gq)
                        for half in range(2):
                            c = c0 + 16 * gq + 8 * half
                            gather(l, idx[:, c:c + 8], half, l or gq or half)
                    continue
                eng.wait_ge(S("idx"), 18 * l + (10, 18)[t])
                if q == 2:
                    eng.wait_ge(S("out"), 16 * 4)
                    ch.add(g.memset(QZ, 0.0))
                    ch.link(g.memset(msk, 0.0))
                    g.affine_select(out=msk[:, 64:128], in_=msk[:, 64:128], compare_op=ALU.is_ge, fill=NEG,
                                    base=-64, pattern=[[0, 64]], channel_multiplier=1).then_inc(S("l1_consts"), 1)
                with eng.Fori(0, n // 16) as i:
                    for half in range(2):
                        gather(l, idx[:, bass.ds(i * 16 + (c0 + 8 * half), 8)], half, True)

        @block.scalar
        def _(eng):
            s = nc.scalar
            ch = Chain(eng, "act_own")
            d = s.dma_start
            par = S("par")
            d(cols[:, :], T["cols"]).then_inc(par, 16)
            d(CSi.rearrange("p a b -> p (a b)"), T["st_conv"]).then_inc(par, 16)
            d(WBA.rearrange("p a b -> p (a b)"), T["wba"]).then_inc(par, 16)
            d(keysT[:, :, :, :].rearrange("p a b c -> p (a b c)"), T["keys"]).then_inc(par, 16)
            d(GW.rearrange("p a b c -> p (a b c)"), T["gw"]).then_inc(par, 16)
            d(S0.rearrange("p a b -> p (a b)"), T["s0"]).then_inc(par, 16)

            def norm(k):
                g, tiles = NORMS[k]
                for i, t in enumerate(tiles):
                    if k == 0:
                        eng.wait_ge(S(f"x_in{t}"), 16)
                    elif k in (1, 3, 5):
                        eng.wait_ge(S("x_mix"), {1: 1, 3: 4, 5: 6}[k] + i)
                    else:
                        eng.wait_ge(S("x_peer"), {2: 1, 4: 3, 6: 4, 7: 6}[k] + i)
                    junk = hT[:, :, 128 * t:128 * t + 128] if k < 2 else hT[:, :, HCOL[t]:HCOL[t] + 128]
                    ch.link(s.activation(junk, X[:, t, :].rearrange("p (a b) -> p a b", b=128), ACT.Square,
                                         accum_out=ssn[:, t:t + 1]))
                    s.activation(rtn[:, t:t + 1], ssn[:, t:t + 1], ACT.Sqrt, bias=EPS, scale=1.0 / D)\
                        .then_inc(S("rms"), 1)

            def evac_hT(k):
                for i, t in enumerate(NORMS[k][1]):
                    eng.wait_ge(S("tr"), NORM_AT[k] + i + 1)
                    c = 128 * t if k < 2 else HCOL[t]
                    s.activation(hT[:, 0:4, c:c + 128],
                                 PS[:, 2 * t, :].rearrange("p (a b) -> p a b", b=128), ACT.Copy).then_inc(S("hT_a"), 1)

            norm(0)
            eng.wait_ge(par, 16 * 6)
            evac_hT(0)

            def post_conv(bb):
                eng.wait_ge(S("conv"), bb + 1)
                if bb < 8:
                    s.activation(QK[:, bb, :], CV[:, bb, :], ACT.Silu).then_inc(S("silu"), 1)
                else:
                    h = bb - 8
                    ch.add(s.activation(VU[:, h:h + 5:4, :], CV[:, bb, 0:NP].rearrange("p (a b) -> p a b", b=128),
                                 ACT.Silu))
                    s.activation(VU[:, 8, 32 * h:32 * h + 32], CV[:, bb, 259:291], ACT.Silu).then_inc(S("silu"), 1)

            for bb in range(24):
                eng.wait_ge(S("blk"), bb + 1)
                bank = PS[:, bb % 4, :]
                if bb < 12 or 16 <= bb < 20:
                    f = bb if bb < 12 else bb - 4
                    ch.add(s.activation(PJ[:, f, 3:259], bank[:, 0:NP], ACT.Copy))
                    s.activation(PJ[:, f, 262:294], bank[:, NP:NT], ACT.Copy).then_inc(S("ev0"), 1)
                elif bb < 16:
                    s.activation(SZ[:, bb - 12, :], bank[:, 0:NT], ACT.Silu).then_inc(S("ev0"), 1)
                else:
                    s.activation(GG[:, bb - 20, :], bank[:, 0:NT], ACT.Gelu_apprx_tanh).then_inc(S("ev0"), 1)
                if 2 <= bb < 14:
                    post_conv(bb - 2)
                if bb in (16, 17):
                    for i in range(4 * (bb - 16), 4 * (bb - 16) + 4):
                        eng.wait_ge(S("l2"), i + 1)
                        sc = 128.0 if i < 4 else 1.0
                        s.activation(RN[:, i, :], PS[:, 4 + i % 4, 0:291], ACT.Sqrt, bias=sc * EPS, scale=sc)\
                            .then_inc(S("l2_sqrt"), 1)
            eng.wait_ge(S("ba"), 1)
            ch.add(s.activation(TH[:, 0:9], BE, ACT.Tanh, scale=0.5))
            ch.add(s.activation(EAL, cols[:, C_AL:C_AL + 9], ACT.Exp))
            s.activation(EX, MN, ACT.Exp).then_inc(S("ba_exp"), 1)
            for i in range(8):
                gt, f = i // 4, i % 4
                eng.wait_ge(S("gmm"), i + 1)
                eng.wait_ge(S("half_b"), 1)
                o = (L1, L2)[gt]
                s.activation(o[:, f, :], PS[:, 4 + i % 2, 0:291], ACT.Tanh, scale=0.5,
                             bias=HB[:, i:i + 1]).then_inc(S("gate_th"), 1)
            eng.wait_ge(S("log_a"), 4)
            ch.add(s.activation(L3, L1, ACT.Exp))
            s.activation(L4, L1, ACT.Tanh).then_inc(S("lru_t"), 1)
            for bt, (u0, u1) in enumerate(BT):
                n = u1 - u0
                eng.wait_ge(S("tds"), bt + 1)
                gcb = PS[:, (0, 3, 6)[bt], 0:128 * n].rearrange("p (a b) -> p a b", b=128)
                s.activation(E[:, u0:u1, :], gcb, ACT.Exp).then_inc(S("expE"), 1)
                if bt == 0:
                    eng.wait_ge(S("gc"), 1)
                    s.activation(EGC, GC, ACT.Exp).then_inc(S("egc"), 1)
                for u in range(u0, u1):
                    ch.add(s.activation(DT[:, u, :], TD[:, u, :], ACT.Exp, bias=NGC[:, u:u + 1]))
                    s.activation(Dm[:, u, :], TS[:, u, :], ACT.Exp, bias=GC[:, u:u + 1]).then_inc(S("expD"), 1)
            for bt, (u0, u1) in enumerate(BT):
                n = u1 - u0
                eng.wait_ge(S("at_mm"), bt + 1)
                s.activation(AT_[:, u0:u1, :], PS[:, (1, 4, 7)[bt], 0:128 * n].rearrange("p (a b) -> p a b", b=128),
                             ACT.Copy).then_inc(S("at"), 1)
            for bt, (u0, u1) in enumerate(BT):
                eng.wait_ge(S("kv_tr"), bt + 1)
                eng.wait_ge(S("aq"), 3)
                kb, vb = ((0, 2), (3, 5), (6, 6))[bt]
                for u in range(u0, u1):
                    c = 128 * (u - u0)
                    cv = c if bt < 2 else 128
                    ch.add(s.activation(KBE[:, u, :], PS[:, kb, c:c + 128], ACT.Copy, scale=BEG[:, u:u + 1]))
                    s.activation(BV[:, u, :], PS[:, vb, cv:cv + 128], ACT.Copy, scale=BE[:, u:u + 1])\
                        .then_inc(S("kbe"), 1)
            for st, name in enumerate(INV):
                if name == "x3":
                    eng.wait_ge(S("lru_q"), 1)
                    s.activation(L4, L4, ACT.Sqrt, scale=-0.5).then_inc(S("lru_sq"), 1)
                for bt, (u0, u1) in enumerate(BT):
                    n = u1 - u0
                    if not INV_A[name]:
                        continue
                    eng.wait_ge(S("inv_mm"), 3 * st + bt + 1)
                    bk = (0, 4, 0)[bt]

                    def cp(dst, i):
                        return s.activation(dst[:, u0:u1, :], PS[:, bk + i, 0:128 * n]
                                            .rearrange("p (a b) -> p a b", b=128), ACT.Copy)
                    if name == "a2":
                        cp(P2, 0).then_inc(S("inv_a"), 1)
                    elif name == "n2":
                        ch.add(cp(P4, 2))
                        cp(P4T, 3).then_inc(S("inv_a"), 1)
                    elif name == "n4":
                        cp(P8T, 2).then_inc(S("inv_a"), 1)
                    else:
                        cp(XM, 0).then_inc(S("inv_a"), 1)
            for bt, (u0, u1) in enumerate(BT):
                n = u1 - u0
                eng.wait_ge(S("w_mm"), bt + 1)
                s.activation(NW[:, u0:u1, :], PS[:, (0, 4, 1)[bt], 0:128 * n].rearrange("p (a b) -> p a b", b=128),
                             ACT.Copy, scale=-1.0).then_inc(S("nw"), 1)
            for bt, bk in ((0, 2), (2, 3), (1, 5)):
                u0, u1 = BT[bt]
                n = u1 - u0
                eng.wait_ge(S("vn_mm"), (0, 2, 1)[bt] + 1)
                if bt == 2:
                    for h in range(4):
                        s.activation(VNm[:, h, :], PS[:, bk, 0:128], ACT.Copy, scale=bm32[:, 32 * h:32 * h + 1])
                s.activation(VN[:, u0:u1, :], PS[:, bk, 0:128 * n].rearrange("p (a b) -> p a b", b=128),
                             ACT.Copy).then_inc(S("vn"), 1)
            for bt, (u0, u1) in enumerate(BT):
                eng.wait_ge(S("o_mm"), (1, 3, 2)[bt])
                for u in range(u0, u1):
                    s.activation(TD[:, u, :], PS[:, (6, 1, 7)[bt], 128 * (u - u0):128 * (u - u0) + 128], ACT.Square,
                                 accum_out=ss[:, u:u + 1]).then_inc(S("o_ss"), 1)
            norm(1)
            evac_hT(1)

            def gate_exp(q):
                eng.wait_ge(S("gmax"), q + 1)
                c0, n = UNITS[q][0], UNITS[q][3]
                s.activation(gate[:, c0:c0 + n], gate[:, c0:c0 + n], ACT.Exp).then_inc(S("gexp"), 1)

            def step(m, i=None):
                eng.wait_ge(S("dots"), at(i, m + 1))
                o = m % UVS
                s.activation(gl[:, o:o + 1], dots[:, o:o + 1], ACT.Gelu_apprx_tanh).then_inc(S("gelu"), 1)

            run = Steps(eng, step)

            def queries(ps, upto):
                nq = (NT, 160, 128)[ps]
                b0 = (B_Q0, B_Q1, B_Q1 + 48)[ps]

                def score(j):
                    eng.wait_ge(S("sc_mm"), 16 * ps + j + 1)
                    bk = PS[:, j % 4, :]
                    h = j // 2
                    q = 32 * (h % 4)
                    if ps < 2:
                        if h >= 4:
                            eng.wait_ge(S("idx"), 18 * ps + h - 3)
                        r = s.activation(SC0[:, j % 8, :], bk[:, 0:128], ACT.Copy)
                        r = s.activation(SCS[q:q + 32, 2 * (h // 4) + j % 2, :], bk[q:q + 32, 256:384], ACT.Copy)
                    if ps != 1:
                        r = s.activation(SC1[:, j, :], bk[:, 128:256], ACT.Copy)
                    r.then_inc(S("sc"), 1)
                for j in range(16):
                    upto("q", j)
                    eng.wait_ge(S("blk"), b0 + j + 1)
                    s.activation(QT[:, j % 4, 0:nq], PS[:, 4 + j % 2, 0:nq], ACT.Copy).then_inc(S("qt"), 1)
                    if j >= 1:
                        score(j - 1)
                score(15)

            eng.wait_ge(S("out"), 16 * 4)
            queries(0, lambda kind, j: None)
            gate_exp(0)
            run.upto(16)
            gate_exp(1)
            run.upto(32)
            run.loop(32, 8)
            gate_exp(2)

            def mixer1(ps):
                def upto(kind, j=0):
                    run.upto(PLAN[ps, kind, j])
                W_ = (128, 256)[ps]
                norm(2 + 2 * ps)
                upto("norm2")
                evac_hT(2 + 2 * ps)
                if ps == 0:
                    eng.wait_ge(S("lam_s"), 1)
                    s.activation(la_[:, 2:4], la_[:, 0:2], ACT.Exp).then_inc(S("lam_e"), 1)
                    eng.wait_ge(S("l1_consts"), 1)
                nq = (160, 128)[ps]
                for j in range(24):
                    upto("qkv", j)
                    eng.wait_ge(S("blk"), B_QKV + 48 * ps + j + 1)
                    bank = PS[:, j % 4, :]
                    if j < 8:
                        s.activation(QZ[0:64, 2 * j, 0:nq], bank[0:64, 0:nq], ACT.Copy, scale=0.125)
                        r = s.activation(QZ[64:128, 2 * j + 1, 0:nq], bank[64:128, 0:nq], ACT.Copy, scale=0.125)
                    elif j < 16:
                        r = s.activation(KTt[:, j - 8, 128 * ps:128 * ps + 128], bank[:, 0:128], ACT.Copy)
                        if ps == 0:
                            r = s.activation(KTt[:, j - 8, NP:NT], bank[:, 128:160], ACT.Copy)
                    elif ps == 0:
                        r = s.activation(Vt[:, 0:3:2, 128 * (j - 16):128 * (j - 16) + 128],
                                         bank[:, 0:256].rearrange("p (t n) -> p t n", t=2), ACT.Copy)
                    else:
                        r = s.activation(Vt[:, 1, 128 * (j - 16):128 * (j - 16) + 128], bank[:, 0:128], ACT.Copy)
                    r.then_inc(S("ev1"), 1)
                for h in range(HC + 2):
                    upto("head", h)
                    if h < HC:
                        q = h % 2
                        eng.wait_ge(S("smax"), 8 * ps + h + 1)
                        for c in range(2):
                            s.activation(PP[:, q, W_ * c:W_ * c + W_], PS[:, q, W_ * c:W_ * c + W_], ACT.Exp,
                                         bias=la_[:, 8 + 2 * q + c:9 + 2 * q + c],
                                         accum_out=la_[:, 24 + 2 * q + c:25 + 2 * q + c]).then_inc(S("sexp"), 1)
                    if 1 <= h <= HC:
                        q = (h - 1) % 2
                        eng.wait_ge(S("p_tr"), 8 * ps + h)
                        s.activation(PTt[:, q, 0:W_], PS[:, 4 + q, 0:W_], ACT.Copy).then_inc(S("pt"), 1)
                for gq in range(2 * (1 - ps)):
                    upto("smp", 2 * gq)
                    eng.wait_ge(S("ssmax"), gq + 1)
                    for c in range(2):
                        s.activation(PPs[:, c, :], PS[:, 2 * c:2 * c + 2, :].rearrange("p a b -> p (a b)")[:, 0:544],
                                     ACT.Exp, bias=la_[:, 40 + c:41 + c], accum_out=la_[:, 44 + c:45 + c])\
                            .then_inc(S("ssexp"), 1)
                    upto("smp", 2 * gq + 1)
                    eng.wait_ge(S("ps_tr"), gq + 1)
                    ch.add(s.activation(PTt.rearrange("p a b -> p (a b)")[:, 0:512], PS[:, 4, :], ACT.Copy))
                    s.activation(PTt.rearrange("p a b -> p (a b)")[0:32, 512:640], PS[0:32, 5, 0:128], ACT.Copy)\
                        .then_inc(S("pts"), 1)
                upto("on")
                nu = (10, 8)[ps]
                eng.wait_ge(S("os_ss"), ps + 1)
                s.activation(rstd[:, 0:nu], ss[:, 0:nu], ACT.Sqrt, bias=EPS, scale=1.0 / 128).then_inc(S("os_rms"), 1)
                for i in range((3, 2)[ps]):
                    eng.wait_ge(S("o_tr"), 3 * ps + i + 1)
                    if i < 2:
                        s.activation(mixT[:, 4 * i:4 * i + 4, 128 * ps:128 * ps + 128],
                                     PS[:, i, :].rearrange("p (a b) -> p a b", b=128), ACT.Copy,
                                     scale=la_[:, 50:51]).then_inc(S("mix1"), 1)
                    else:
                        for gq in range(2):
                            for r in range(4):
                                s.activation(mixT[:, 4 * gq:4 * gq + 4, NP + 32 * r:NP + 32 * r + 32],
                                             PS[:, 4, 128 * gq:128 * gq + 128].rearrange("p (a b) -> p a b", b=32),
                                             ACT.Copy, scale=la_[:, 50:51]).then_inc(S("mix1"), 1)
                for j in range(8):
                    upto("out", j)
                norm(3 + 2 * ps)
                upto("norm3")
                evac_hT(3 + 2 * ps)
                queries(1 + ps, upto)

            mixer1(0)
            gate_exp(3)
            run.upto(AHEAD)
            gate_exp(4)
            mixer1(1)
            run.upto(448)
            gate_exp(5)
            norm(6)
            run.loop(448, 8)
            norm(7)

        @block.vector
        def _(eng):
            v = nc.vector
            ch = Chain(eng, "dve_own")

            def rsqrt(r, root, sq, n):
                w = nwt[:, 0:r.shape[1]]
                ch.settle()
                ch.link(v.reciprocal(r, root))
                ch.add(v.tensor_scalar(sq, sq, 1.0 / n, EPS, ALU.mult, ALU.add))
                ch.link(v.tensor_tensor(w, r, r, ALU.mult))
                ch.link(v.tensor_tensor(w, w, sq, ALU.mult))
                ch.link(v.tensor_scalar(w, w, -0.5, 1.5, ALU.mult, ALU.add))
                ch.link(v.tensor_tensor(r, r, w, ALU.mult))

            def norm(k, last=False, between=lambda: None):
                tiles = NORMS[k][1]
                for i, t in enumerate(tiles):
                    eng.wait_ge(S("rms"), NORM_AT[k] + i + 1)
                    rsqrt(rsn[:, t:t + 1], rtn[:, t:t + 1], ssn[:, t:t + 1], D)
                    eng.wait_ge(S("gain"), 16 * (GAIN_LOAD[k] + 1))
                    v.scalar_tensor_tensor(out=Hn[:, t, :], in0=X[:, t, :], scalar=rsn[:, t:t + 1], in1=gB[:, :],
                                           op0=ALU.mult, op1=ALU.mult).then_inc(S("Hn"), 1)
                if last:
                    return
                between()
                for i, t in enumerate(tiles):
                    eng.wait_ge(S("tr"), NORM_AT[k] + i + 1)
                    c = 128 * t if k < 2 else HCOL[t]
                    v.tensor_copy(hT[:, 4:8, c:c + 128],
                                  PS[:, 2 * t + 1, :].rearrange("p (a b) -> p a b", b=128)).then_inc(S("hT_v"), 1)

            norm(0)
            eng.wait_ge(S("ba_mm"), 1)
            eng.wait_ge(S("par"), 16 * 6)
            ch.link(v.tensor_copy(BA, PS[:, 4, 0:24]))
            ba = BA.rearrange("p (t c) -> p t c", c=8)
            ch.add(v.tensor_copy(BE[:, 0:8].rearrange("p (t c) -> p t c", c=4), ba[:, 0:2, 0:4]))
            ch.add(v.tensor_tensor(AL[:, 0:8].rearrange("p (t c) -> p t c", c=4), ba[:, 0:2, 4:8],
                            cols[:, C_DT:C_DT + 8].rearrange("p (t c) -> p t c", c=4), ALU.add))
            for h in range(4):
                r = slice(32 * h, 32 * h + 32)
                ch.add(v.tensor_copy(BE[r, 8:9], BA[r, 16 + h:17 + h]))
                ch.add(v.tensor_tensor(AL[r, 8:9], BA[r, 20 + h:21 + h], cols[r, C_DT + 8:C_DT + 9], ALU.add))
            ch.add(v.tensor_scalar(AL[:, 9:13], cols[:, C_LM:C_LM + 4], -1.0, None, ALU.mult))
            v.tensor_scalar(HB, cols[:, C_GA:C_GA + 8], 0.5, None, ALU.mult).then_inc(S("half_b"), 1)
            ch.settle()
            ch.link(v.tensor_scalar(SR, AL, -1.0, None, ALU.mult))
            v.tensor_tensor(MN, AL, SR, ALU.min).then_inc(S("ba"), 1)

            def conv(f):
                w = lambda j: cols[:, C_CW + 4 * f + j:C_CW + 4 * f + j + 1]
                if f < 12:
                    ch.link(v.tensor_scalar(CV[:, f, :], PJ[:, f, 0:291], w(0), None, ALU.mult))
                else:
                    ch.link(v.tensor_scalar(CV[:, f, :], PJ[:, f, 0:291], w(0), cols[:, C_CB + f - 12:C_CB + f - 11],
                                            ALU.mult, ALU.add))
                for j in (1, 2):
                    ch.link(v.scalar_tensor_tensor(out=CV[:, f, :], in0=PJ[:, f, j:j + 291], scalar=w(j),
                                                   in1=CV[:, f, :], op0=ALU.mult, op1=ALU.add))
                v.scalar_tensor_tensor(out=CV[:, f, :], in0=PJ[:, f, 3:294], scalar=w(3), in1=CV[:, f, :],
                                       op0=ALU.mult, op1=ALU.add).then_inc(S("conv"), 1)

            eng.wait_ge(S("consts"), 1)
            for f in range(12):
                eng.wait_ge(S("ev0"), f + 1)
                conv(f)
            for i in range(8):
                eng.wait_ge(S("l2_sqrt"), i + 1)
                ch.link(v.reciprocal(RN[:, i, :], RN[:, i, :]))
                o, h = (QU, KU)[i // 4], i % 4
                two = lambda t: t[:, i, 0:NP].rearrange("p (a b) -> p a b", b=128)
                ch.add(v.tensor_tensor(o[:, h:h + 5:4, :], two(QK), two(RN), ALU.mult))
                v.tensor_tensor(o[:, 8, 32 * h:32 * h + 32], QK[:, i, 259:291], RN[:, i, 259:291], ALU.mult)\
                    .then_inc(S("qu"), 1)
            for f in range(12, 16):
                eng.wait_ge(S("ev0"), f + 4 + 1)
                conv(f)
            eng.wait_ge(S("ba_exp"), 1)
            ch.link(v.tensor_scalar(SR, EX, 2.0, None, ALU.add))
            ch.link(v.reciprocal(SR, SR))
            ch.link(v.tensor_tensor(SR, SR, EX, ALU.mult))
            ch.link(v.tensor_tensor(SQ_, SR, SR, ALU.mult))
            ch.link(v.tensor_scalar(PL, SQ_, 1.0 / 17, None, ALU.mult))
            for k in (15, 13, 11, 9, 7, 5, 3):
                ch.link(v.scalar_tensor_tensor(out=PL, in0=PL, scalar=1.0 / k, in1=SQ_, op0=ALU.add, op1=ALU.mult))
            ch.link(v.scalar_tensor_tensor(out=PL, in0=PL, scalar=1.0, in1=SR, op0=ALU.add, op1=ALU.mult))
            ch.link(v.tensor_scalar(SP, AL, 0.0, None, ALU.max))
            ch.link(v.scalar_tensor_tensor(out=SP, in0=PL, scalar=2.0, in1=SP, op0=ALU.mult, op1=ALU.add))
            ch.add(v.tensor_scalar(CLM, SP[:, 9:13], -4.0, None, ALU.mult))
            ch.add(v.tensor_scalar(BE, TH[:, 0:9], 0.5, 0.5, ALU.mult, ALU.add))
            v.scalar_tensor_tensor(out=G9, in0=SP[:, 0:9], scalar=-1.0, in1=EAL, op0=ALU.mult, op1=ALU.mult)\
                .then_inc(S("softplus"), 1)
            eng.wait_ge(S("gc_mm"), 1)
            ch.link(v.tensor_copy(GC, PS[:, 7, 0:9]))
            v.tensor_scalar(NGC, GC, -1.0, None, ALU.mult).then_inc(S("gc"), 1)
            for bt, (u0, u1) in enumerate(BT):
                n = u1 - u0
                if bt < 2:
                    eng.wait_ge(S("gcB"), bt + 1)
                else:
                    eng.wait_ge(S("kk"), 3)
                gcb = PS[:, (0, 3, 6)[bt], 0:128 * n].rearrange("p (a b) -> p a b", b=128)
                mt, ms = ((MDT, MDs), (MDT, MDs), (MDTs, MDss))[bt]
                bc = lambda m: m.unsqueeze(1).to_broadcast([128, n, 128])
                ch.add(v.tensor_tensor(TD[:, u0:u1, :], gcb, bc(mt), ALU.add))
                v.scalar_tensor_tensor(out=TS[:, u0:u1, :], in0=gcb, scalar=-1.0, in1=bc(ms), op0=ALU.mult,
                                       op1=ALU.add).then_inc(S("tds"), 1)
            eng.wait_ge(S("egc"), 1)
            ch.link(v.tensor_tensor(BEG, BE, EGC, ALU.mult))
            for bt, (u0, u1) in enumerate(BT):
                n = u1 - u0
                eng.wait_ge(S("expE"), bt + 1)
                eng.wait_ge(S("expD"), u1)
                if bt < 2:
                    ch.add(v.tensor_copy(EGL[:, u0:u1], E[:, u0:u1, 127:128].rearrange("p a b -> p (a b)")))
                    r = v.tensor_copy(DEC[:, u0:u1], DT[:, u0:u1, 127:128].rearrange("p a b -> p (a b)"))
                else:
                    ch.add(v.tensor_copy(egls, E[:, 8, 31:128:32]))
                    r = v.tensor_reduce(DEC[:, 8:9], DT[:, 8, 31:128:32], AX.X, ALU.add)
                r.then_inc(S("egl"), 1)
                kk = PS[:, (1, 4, 6)[bt], :]
                c0 = (0, 0, 128)[bt]
                eng.wait_ge(S("kk"), bt + 1)
                for u in range(u0, u1):
                    c = c0 + 128 * (u - u0)
                    v.scalar_tensor_tensor(out=Am[:, u, :], in0=kk[:, c:c + 128], scalar=BE[:, u:u + 1],
                                           in1=Dm[:, u, :], op0=ALU.mult, op1=ALU.mult).then_inc(S("A"), 1)
                qk = PS[:, (2, 5, 6)[bt], :]
                eng.wait_ge(S("egl"), bt + 1)
                c0 = (0, 0, 256)[bt]
                v.tensor_tensor(DT[:, u0:u1, :], qk[:, c0:c0 + 128 * n].rearrange("p (a b) -> p a b", b=128),
                                DT[:, u0:u1, :], ALU.mult).then_inc(S("aq"), 1)
            eng.wait_ge(S("egl"), 3)
            for bt, (u0, u1) in enumerate(BT):
                n = u1 - u0
                eng.wait_ge(S("kv_tr"), bt + 1)
                kb = (0, 3, 6)[bt]
                eng.wait_ge(S("kbe"), u1)
                ch.add(v.tensor_tensor(KDEC[:, u0:u1, :], PS[:, kb, 0:128 * n].rearrange("p (a b) -> p a b", b=128),
                                DEC[:, u0:u1].unsqueeze(2).to_broadcast([128, n, 128]), ALU.mult))
                bc = lambda m: m[:, :].unsqueeze(1).to_broadcast([128, n, 128])
                eng.wait_ge(S("at"), bt + 1)
                ch.add(v.tensor_tensor(P1[:, u0:u1, :], Am[:, u0:u1, :], bc(bm16), ALU.mult))
                ch.link(v.tensor_tensor(P1T[:, u0:u1, :], AT_[:, u0:u1, :], bc(bm16), ALU.mult))
                ch.add(v.scalar_tensor_tensor(out=Tm[:, u0:u1, :], in0=P1[:, u0:u1, :], scalar=-1.0, in1=bc(ident),
                                       op0=ALU.mult, op1=ALU.add))
                v.scalar_tensor_tensor(out=TTm[:, u0:u1, :], in0=P1T[:, u0:u1, :], scalar=-1.0, in1=bc(ident),
                                       op0=ALU.mult, op1=ALU.add).then_inc(S("t0"), 1)
            for st, name in enumerate(INV):
                if 1 <= st <= 4:
                    eng.wait_ge(S("lru_den"), 1)
                    v.reciprocal(L1[:, st - 1, :], L1[:, st - 1, :]).then_inc(S("lru_rec"), 1)
                for bt, (u0, u1) in enumerate(BT):
                    n = u1 - u0
                    if not INV_V[name]:
                        continue
                    eng.wait_ge(S("inv_mm"), 3 * st + bt + 1)
                    bk = (0, 4, 0)[bt]
                    src = lambda i: PS[:, bk + i, 0:128 * n].rearrange("p (a b) -> p a b", b=128)
                    if name == "a2":
                        v.tensor_copy(P2T[:, u0:u1, :], src(1)).then_inc(S("inv_v"), 1)
                        continue
                    op = ALU.add if name[0] == "n" else ALU.subtract
                    if name != "m3":
                        ch.add(v.tensor_tensor(Tm[:, u0:u1, :], Tm[:, u0:u1, :], src(0), op))
                    v.tensor_tensor(TTm[:, u0:u1, :], TTm[:, u0:u1, :], src(1), op).then_inc(S("inv_v"), 1)
            eng.wait_ge(S("s_mm"), 1)
            v.tensor_copy(S1, PS[:, 4, :].rearrange("p (a b) -> p a b", b=128)).then_inc(S("s1"), 1)
            eng.wait_ge(S("s_mm"), 2)
            for h in range(4):
                r = v.scalar_tensor_tensor(out=S0[:, h, :], in0=S0[:, h, :], scalar=egls[:, h:h + 1],
                                           in1=PS[:, 0, 128 * h:128 * h + 128], op0=ALU.mult, op1=ALU.add)
            r.then_inc(S("sfin"), 1)
            eng.wait_ge(S("s_mm"), 3)
            for h in range(4):
                r = v.scalar_tensor_tensor(out=S2[:, h, :], in0=S1[:, h, :], scalar=EGL[:, 4 + h:5 + h],
                                           in1=PS[:, 4, 128 * h:128 * h + 128], op0=ALU.mult, op1=ALU.add)
            r.then_inc(S("sfin"), 1)
            eng.wait_ge(S("lru_u"), 1)
            for f in range(4):
                ch.add(v.tensor_tensor_scan(L1[:, f, 0:NP], L3[:, f, 0:NP], L2[:, f, 0:NP], 0.0, ALU.mult, ALU.add))
                r = v.tensor_tensor_scan(L1[:, f, 259:291], L3[:, f, 259:291], L2[:, f, 259:291],
                                         cols[:, C_H0 + f:C_H0 + f + 1], ALU.mult, ALU.add)
            r.then_inc(S("hs"), 1)
            for bt, (u0, u1) in enumerate(BT):
                n = u1 - u0
                eng.wait_ge(S("o_rs"), bt + 1)
                v.tensor_tensor(ON[:, u0:u1, :], PS[:, (6, 1, 7)[bt], 0:128 * n].rearrange("p (a b) -> p a b", b=128),
                                rstd[:, u0:u1].unsqueeze(2).to_broadcast([128, n, 128]), ALU.mult)\
                    .then_inc(S("on"), 1)
            for bt, (u0, u1) in enumerate(BT):
                eng.wait_ge(S("on_tr"), bt + 1)
                if bt < 2:
                    ch.add(v.scalar_tensor_tensor(out=mixT[:, 0:4, 128 * bt:128 * bt + 128],
                                           in0=PS[:, (2, 3)[bt], :].rearrange("p (a b) -> p a b", b=128),
                                           scalar=cols[:, C_AN:C_AN + 1], in1=SZ[:, :, 128 * bt:128 * bt + 128],
                                           op0=ALU.mult, op1=ALU.mult))
                else:
                    for r in range(4):
                        last = v.scalar_tensor_tensor(out=mixT[:, 0:4, NP + 32 * r:NP + 32 * r + 32],
                                                      in0=PS[:, 5, 0:128].rearrange("p (a b) -> p a b", b=32),
                                                      scalar=cols[:, C_AN:C_AN + 1], in1=SZ[:, :, NP:NT],
                                                      op0=ALU.mult, op1=ALU.mult)
            last.then_inc(S("mix_d"), 1)

            def residual(ps, upto=lambda kind, j: None):
                for half in range(2):
                    for j in range(4):
                        upto("out", 4 * half + j)
                    eng.wait_ge(S("blk"), (B_OUT0, B_OUT1, B_OUT1 + 48)[ps] + 4 * half + 4)
                    for t in ((0, 1, 2), (2, 0), (1,))[ps]:
                        o = X[:, t, 512 * half:512 * half + 512]
                        r = v.tensor_tensor(o, o, PS[:, 2 * t + half, :], ALU.add)
                        if half:
                            r.then_inc(S("x_mix"), 1)
                        else:
                            ch.add(r)
                ch.settle()

            residual(0)
            norm(1)

            def top16(n, src, tmp, val, ind):
                for i in range(n):
                    ch.add(v.max(val(i)[:, 0:8], src(i)))
                ch.settle()
                for i in range(n):
                    ch.add(v.max_index(ind(i)[:, 0:8], val(i)[:, 0:8], src(i)))
                    ch.add(v.match_replace(tmp(i), val(i)[:, 0:8], src(i), -3.0e38))
                ch.settle()
                for i in range(n):
                    ch.add(v.max(val(i)[:, 8:16], tmp(i)))
                ch.settle()
                for i in range(n):
                    ch.add(v.max_index(ind(i)[:, 8:16], val(i)[:, 8:16], tmp(i)))

            def pick(sc, idx_to, gate_to):
                top16(2, lambda c: sc[:, c, :], lambda c: tm[:, c, :], lambda c: pv_[:, c, :], lambda c: pi[:, c, :])
                ch.settle()
                ch.link(v.tensor_tensor(cand, pv_[:, 0, :].unsqueeze(2).to_broadcast([128, 16, 16]),
                                        pv_[:, 1, :].unsqueeze(1).to_broadcast([128, 16, 16]), ALU.add))
                flat = cand.rearrange("p a b -> p (a b)")
                top16(1, lambda i: flat, lambda i: candt, lambda i: tv, lambda i: sel)
                ch.settle()
                ch.add(v.tensor_copy(gate_to, tv))
                ch.add(v.tensor_scalar(ab[:, 0:16], sel, 4, None, ALU.logical_shift_right))
                ch.link(v.tensor_scalar(ab[:, 16:32], sel, 15, None, ALU.bitwise_and))
                ch.link(v.tensor_tensor(hot, ab.unsqueeze(2).to_broadcast([128, 32, 16]),
                                        iota16[:, :].unsqueeze(1).to_broadcast([128, 32, 16]), ALU.is_equal))
                h4 = hot.rearrange("p (c k) n -> p c k n", c=2)
                ch.link(v.tensor_tensor(h4, h4, pi.unsqueeze(2).to_broadcast([128, 2, 16, 16]), ALU.mult))
                ch.link(v.tensor_reduce(i12, hot, AX.X, ALU.add))
                v.scalar_tensor_tensor(out=idx_to, in0=i12[:, 0:16], scalar=float(NKEY), in1=i12[:, 16:32],
                                       op0=ALU.mult, op1=ALU.add).then_inc(S("idx"), 1)

            def gate_of(q):
                c0, n = UNITS[q][0], UNITS[q][3]
                nh = n // 16
                ch.settle()
                gt = gate[:, c0:c0 + n].rearrange("p (h s) -> p h s", s=16)
                top = gsum[:, 0:nh].unsqueeze(2)
                ch.link(v.tensor_copy(top, gt[:, :, 0:1]))
                v.tensor_tensor(gt, gt, top.to_broadcast([128, nh, 16]), ALU.subtract).then_inc(S("gmax"), 1)
                eng.wait_ge(S("gexp"), q + 1)
                ch.link(v.tensor_reduce(gsum[:, 0:nh], gt, AX.X, ALU.add))
                ch.link(v.reciprocal(gsum[:, 0:nh], gsum[:, 0:nh]))
                ch.link(v.tensor_tensor(gt, gt, top.to_broadcast([128, nh, 16]), ALU.mult))

            def step(m, i=None):
                q = max(k for k in range(6) if UNITS[k][2] <= m)
                c0, xt, m0, _ = UNITS[q]
                c, sl = m % 16, m % UVS
                if c == 0:
                    g0 = c0 + m - m0
                    v.tensor_copy(gst[:, :], gate[:, g0:g0 + 16] if i is None else gate[:, bass.ds(i * 16 + g0, 16)])\
                        .then_inc(S("gates"), 1)
                    eng.wait_ge(S("gates"), m // 16 + 1 if i is None else i + (m // 16 + 1))
                landed = 16 * (m // UVS + 1)
                eng.wait_ge(S(f"uv_in{sl}"), landed if i is None else i * 32 + landed)
                v.tensor_tensor_reduce(UV[:, sl, 0:D], UV[:, sl, 0:D], Hn[:, xt, :], 1.0, 0.0,
                                       ALU.mult, ALU.add, dots[:, sl:sl + 1]).then_inc(S("dots"), 1)
                eng.wait_ge(S("gelu"), at(i, m + 1))
                v.tensor_scalar(DG[:, sl, :], ident[:, :], gl[:, sl:sl + 1], gst[:, c:c + 1],
                                ALU.mult, ALU.mult).then_inc(S("diag"), 1)
                if c == 15:
                    eng.wait_ge(S("diag"), at(i, m + 1))

            def end(q):
                xt = UNITS[q][1]
                if xt == 2:
                    eng.wait_ge(S("acc"), ACC[q] - 1)
                    for half in range(2):
                        v.tensor_copy(YS[:, 512 * half:512 * half + 512], PS[:, 6 + half, :]).then_inc(S("ys"), 1)
                eng.wait_ge(S("acc"), ACC[q])
                for half in range(2):
                    o = X[:, xt, 512 * half:512 * half + 512]
                    r = v.tensor_tensor(o, o, PS[:, 6 + half, :], ALU.add)
                    if half:
                        r.then_inc(S("x_peer"), 1)

            run = Steps(eng, step, end=end)

            def picks(ps, upto):
                def tile0(h):
                    eng.wait_ge(S("sc"), 16 * ps + 2 * h + 2)
                    r = 2 * (h % 4)
                    pick(SC0[:, r:r + 2, :], idx[:, 16 * h:16 * h + 16], gate[:, 16 * h:16 * h + 16])

                def tile1(h):
                    eng.wait_ge(S("sc"), 16 * ps + 2 * h + 2)
                    c = 128 + 16 * h
                    pick(SC1[:, 2 * h:2 * h + 2, :], idx[:, c:c + 16], gate[:, c:c + 16])

                def sample(gq):
                    eng.wait_ge(S("sc"), 16 * ps + 8 * gq + 8)
                    c = 256 + 16 * gq
                    pick(SCS[:, 2 * gq:2 * gq + 2, :], idx[:, c:c + 16], gate[:, c:c + 16])

                for h in range(PH):
                    for j in range(2 * h, 2 * h + 2):
                        upto("q", j)
                    if h == 0:
                        continue
                    if ps < 2:
                        if h == 5:
                            sample(0)
                        if h < 7:
                            tile0(h - 1)
                    else:
                        tile1(h - 1)
                if ps < 2:
                    sample(1)
                    gate_of(3 * ps)
                    upto("q", 16)
                    tile0(6)
                    upto("q", 17)
                    tile0(7)
                else:
                    tile1(7)

            def pick_tile1(i):
                ch.loop()
                ch.link(v.tensor_copy(rows.rearrange("p a b -> p (a b)"),
                                      SC1.rearrange("p a b -> p (a b)")[:, bass.ds(i * 2 * NKEY, 2 * NKEY)]))
                pick(rows, idx[:, bass.ds(i * 16 + 128, 16)], gate[:, bass.ds(i * 16 + 128, 16)])
                ch.loop_end()

            picks(0, lambda kind, j: run.upto({16: 8, 17: 16}.get(j, 0)))
            gate_of(1)
            run.upto(32)
            run.loop(32, 8, pick_tile1)
            gate_of(2)

            def mixer1(ps):
                def upto(kind, j=0):
                    run.upto(PLAN[ps, kind, j])
                W_ = (128, 256)[ps]
                norm(2 + 2 * ps, between=lambda: upto("norm2"))
                NL = la_[:, 4:5]
                if ps == 0:
                    eng.wait_ge(S("lq"), 16)
                    ch.link(v.tensor_tensor(lq[:, 0:2, :], lq[:, 0:2, :], lq[:, 2:4, :], ALU.mult))
                    v.tensor_reduce(la_[:, 0:2], lq[:, 0:2, :], AX.X, ALU.add).then_inc(S("lam_s"), 1)
                    ch.link(v.tensor_scalar(la_[:, 50:51], cols[:, C_CN:C_CN + 1], 1.0 - LAM_INIT, None, ALU.mult))
                    eng.wait_ge(S("lam_e"), 1)
                    ch.link(v.tensor_tensor(la_[:, 4:5], la_[:, 3:4], la_[:, 2:3], ALU.subtract))
                    ch.link(v.tensor_scalar(NL, NL, -LAM_INIT, None, ALU.add))
                for j in range(24):
                    upto("qkv", j)
                OS = Hn[:, ps, :].rearrange("p (a b) -> p a b", b=128)
                OSs = Hn[:, 2, 0:256].rearrange("p (a b) -> p a b", b=128)
                for h in range(HC + 2):
                    upto("head", h)
                    if h < HC:
                        q = h % 2
                        eng.wait_ge(S("s_qk"), 8 * ps + h + 1)
                        v.tensor_reduce(la_[:, 8 + 2 * q:10 + 2 * q],
                                        PS[:, q, 0:2 * W_].rearrange("p (c n) -> p c n", c=2), AX.X, ALU.max,
                                        negate=True).then_inc(S("smax"), 1)
                    if 1 <= h <= HC:
                        q = (h - 1) % 2
                        L = la_[:, 24 + 2 * q:26 + 2 * q]
                        eng.wait_ge(S("sexp"), 16 * ps + 2 * h)
                        ch.link(v.reciprocal(L, L))
                        ch.add(v.tensor_scalar(L[:, 1:2], L[:, 1:2], NL, None, ALU.mult))
                        ch.link(v.tensor_scalar(PC[:, q, 0:W_], PP[:, q, 0:W_], L[:, 0:1], None, ALU.mult))
                        v.scalar_tensor_tensor(out=PC[:, q, 0:W_], in0=PP[:, q, W_:2 * W_], scalar=L[:, 1:2],
                                               in1=PC[:, q, 0:W_], op0=ALU.mult, op1=ALU.add).then_inc(S("pc"), 1)
                    if h in (5, 9):
                        i = h // 9
                        eng.wait_ge(S("pv"), 8 * ps + 4 * i + 4)
                        v.tensor_copy(OS[:, 4 * i:4 * i + 4, :], PS[:, 2 + i, :].rearrange("p (a b) -> p a b", b=128))\
                            .then_inc(S("os"), 1)
                for gq in range(2 * (1 - ps)):
                    upto("smp", 2 * gq)
                    eng.wait_ge(S("s_qks"), gq + 1)
                    v.tensor_reduce(la_[:, 40:42], PS[:, 0:4, :].rearrange("p (c a) b -> p c (a b)", c=2)[:, :, 0:544],
                                    AX.X, ALU.max, negate=True).then_inc(S("ssmax"), 1)
                    L = la_[:, 44:46]
                    eng.wait_ge(S("ssexp"), 2 * gq + 2)
                    ch.link(v.reciprocal(L, L))
                    ch.add(v.tensor_scalar(L[:, 1:2], L[:, 1:2], NL, None, ALU.mult))
                    ch.link(v.tensor_scalar(PCs[:, 0, :], PPs[:, 0, :], L[:, 0:1], None, ALU.mult))
                    v.scalar_tensor_tensor(out=PCs[:, 0, :], in0=PPs[:, 1, :], scalar=L[:, 1:2], in1=PCs[:, 0, :],
                                           op0=ALU.mult, op1=ALU.add).then_inc(S("pcs"), 1)
                    upto("smp", 2 * gq + 1)
                    eng.wait_ge(S("pvs"), gq + 1)
                    v.tensor_copy(OSs[:, gq, :], PS[:, 5, 128:256]).then_inc(S("os"), 1)
                upto("on")
                eng.wait_ge(S("os"), (4, 6)[ps])
                parts = ((OS, 0, 8), (OSs, 8, 10))[0:2 - ps]
                for o, u0, u1 in parts:
                    ch.add(v.tensor_tensor(sqs[:, u0:u1, :], o, o, ALU.mult))
                ch.settle()
                nu = (10, 8)[ps]
                v.tensor_reduce(ss[:, 0:nu], sqs[:, 0:nu, :], AX.X, ALU.add).then_inc(S("os_ss"), 1)
                eng.wait_ge(S("os_rms"), ps + 1)
                rsqrt(rstd[:, 0:nu], rstd[:, 0:nu], ss[:, 0:nu], 128)
                for o, u0, u1 in parts:
                    r = v.tensor_tensor(o, o, rstd[:, u0:u1].unsqueeze(2).to_broadcast([128, u1 - u0, 128]), ALU.mult)
                r.then_inc(S("os_n"), 1)
                residual(1 + ps, upto)
                norm(3 + 2 * ps, between=lambda: upto("norm3"))
                picks(1 + ps, upto)

            mixer1(0)
            run.upto(AHEAD)
            gate_of(4)
            mixer1(1)
            run.upto(448)
            gate_of(5)
            norm(6, last=True)
            run.loop(448, 8)
            norm(7, last=True)

        @block.tensor
        def _(eng):
            t_ = nc.tensor
            mm = t_.matmul

            def transposes(k):
                for i, t in enumerate(NORMS[k][1]):
                    eng.wait_ge(S("Hn"), NORM_AT[k] + i + 1)
                    for c in range(KT):
                        r = t_.transpose(PS[:, 2 * t + c // 4, 128 * (c % 4):128 * (c % 4) + 128],
                                         Hn[:, t, 128 * c:128 * c + 128], ident[:, :])
                    r.then_inc(S("tr"), 1)
                eng.wait_ge(S("hT_a"), NORM_AT[k + 1])
                eng.wait_ge(S("hT_v"), NORM_AT[k + 1])

            def landed(bb):
                eng.wait_ge(S(f"w_in{bb % WSLOTS}"), 16 * (bb // WSLOTS + 1))

            def block_fm(bb, bank, c0=0, n=NT):
                landed(bb)
                for k in range(KT):
                    r = mm(PS[:, bank, 0:n], blkw(bb % WSLOTS, k), hT[:, k, c0:c0 + n], start=(k == 0),
                           stop=(k == KT - 1))
                r.then_inc(S("blk"), 1)

            eng.wait_ge(S("ident"), 1)
            transposes(0)
            for t in range(3):
                for k in range(KT):
                    r = mm(PS[:, 4, 8 * t:8 * t + 8], hT[:, k, 128 * t:128 * t + 128], WBA[:, k, :],
                           start=(k == 0), stop=(k == KT - 1))
            r.then_inc(S("ba_mm"), 1)
            for bb in range(24):
                if bb >= 4:
                    eng.wait_ge(S("ev0"), bb - 3)
                block_fm(bb, bb % 4)
                if bb == 15:
                    eng.wait_ge(S("consts"), 1)
                if bb in (15, 16):
                    for i in range(4 * (bb - 15), 4 * (bb - 15) + 4):
                        eng.wait_ge(S("qk_sq"), i + 1)
                        if i >= 4:
                            eng.wait_ge(S("l2_sqrt"), i - 3)
                        else:
                            eng.wait_ge(S("ba"), 1)
                        mm(PS[:, 4 + i % 4, 0:291], ones[:, :], RN[:, i, :], start=True, stop=True)\
                            .then_inc(S("l2"), 1)
            eng.wait_ge(S("l2_sqrt"), 8)
            eng.wait_ge(S("conv"), 16)
            for i in range(8):
                if i >= 2:
                    eng.wait_ge(S("gate_th"), i - 1)
                mm(PS[:, 4 + i % 2, 0:291], GW[:, i // 4, i % 4, :], CV[:, 12 + i % 4, :], start=True, stop=True)\
                    .then_inc(S("gmm"), 1)
            eng.wait_ge(S("softplus"), 1)
            eng.wait_ge(S("gate_th"), 8)
            eng.wait_ge(S("ev0"), 24)
            mm(PS[:, 7, 0:8], LTp, G9[:, 0:8], start=True, stop=True)
            mm(PS[:, 7, 8:9], LTs, G9[:, 8:9], start=True, stop=True).then_inc(S("gc_mm"), 1)
            eng.wait_ge(S("qu"), 8)
            for bt, (u0, u1) in enumerate(BT):
                b0 = (0, 3, 6)[bt]
                for u in range(u0, u1):
                    c = 128 * (u - u0)
                    r = mm(PS[:, b0, c:c + 128], G9[:, u:u + 1].to_broadcast([128, 128]), LTp if bt < 2 else LTs,
                           start=True, stop=True)
                if bt < 2:
                    r.then_inc(S("gcB"), 1)
                for u in range(u0, u1):
                    c = 128 * (u - u0)
                    o = PS[:, b0 + 1, c:c + 128] if bt < 2 else PS[:, 6, 128:256]
                    mm(o, KU[:, u, :], KU[:, u, :], start=True, stop=True)
                for u in range(u0, u1):
                    c = 128 * (u - u0)
                    o = PS[:, b0 + 2, c:c + 128] if bt < 2 else PS[:, 6, 256:384]
                    r = mm(o, KU[:, u, :], QU[:, u, :], start=True, stop=True)
                r.then_inc(S("kk"), 1)
            for bt, (u0, u1) in enumerate(BT):
                eng.wait_ge(S("A"), u1)
                if bt == 2:
                    eng.wait_ge(S("gc"), 1)
                for u in range(u0, u1):
                    c = 128 * (u - u0)
                    r = t_.transpose(PS[:, (1, 4, 7)[bt], c:c + 128], Am[:, u, :], ident[:, :])
                r.then_inc(S("at_mm"), 1)
            eng.wait_ge(S("silu"), 12)
            for bt, (u0, u1) in enumerate(BT):
                eng.wait_ge(S("aq"), bt + 1)
                eng.wait_ge(S("expE"), bt + 1)
                eng.wait_ge(S("tds"), bt + 1)
                kb, vb = ((0, 2), (3, 5), (6, 6))[bt]
                for u in range(u0, u1):
                    c = 128 * (u - u0)
                    cv = c if bt < 2 else 128
                    t_.transpose(PS[:, kb, c:c + 128], KU[:, u, :], ident[:, :])
                    r = t_.transpose(PS[:, vb, cv:cv + 128], VU[:, u, :], ident[:, :])
                r.then_inc(S("kv_tr"), 1)
            for st, name in enumerate(INV):
                for bt, (u0, u1) in enumerate(BT):
                    bk = (0, 4, 0)[bt]
                    if st == 0:
                        eng.wait_ge(S("t0"), bt + 1)
                        eng.wait_ge(S("kbe"), 9)
                        eng.wait_ge(S("at"), 3)
                    else:
                        eng.wait_ge(S("inv_a"), inv_count(INV_A, st - 1, bt))
                        eng.wait_ge(S("inv_v"), inv_count(INV_V, st - 1, bt))
                    if name == "x1":
                        eng.wait_ge(S("bmT"), 3)
                    if bt == 0 and st:
                        eng.wait_ge(S("inv_a"), inv_count(INV_A, st - 1, 2))
                        eng.wait_ge(S("inv_v"), inv_count(INV_V, st - 1, 2))
                    if bt == 2:
                        if INV_A[name]:
                            eng.wait_ge(S("inv_a"), inv_count(INV_A, st, 0))
                        if INV_V[name]:
                            eng.wait_ge(S("inv_v"), inv_count(INV_V, st, 0))
                    prods = {
                        "a2": ((P1T, P1), (P1, P1T)),
                        "n2": ((P2T, Tm), (Tm, P2T), (P2T, P2), (P2, P2T)),
                        "n4": ((P4T, Tm), (Tm, P4T), (P4, P4T)),
                        "n8": ((P8T, Tm), (Tm, P8T)),
                        "x1": ((B1T, Tm),), "x2": ((B2T, Tm),), "x3": ((B3T, Tm),),
                        "m1": ((TTm, XM), (XM, TTm)), "m2": ((TTm, XM), (XM, TTm)), "m3": (None, (XM, TTm)),
                    }[name]
                    for i, pr in enumerate(prods):
                        if pr is None:
                            continue
                        for u in range(u0, u1):
                            c = 128 * (u - u0)
                            r = mm(PS[:, bk + i, c:c + 128], pr[0][:, u, :], pr[1][:, u, :], start=True, stop=True)
                    r.then_inc(S("inv_mm"), 1)
            eng.wait_ge(S("inv_v"), inv_count(INV_V, len(INV) - 1, 2))
            for bt, (u0, u1) in enumerate(BT):
                for u in range(u0, u1):
                    c = 128 * (u - u0)
                    r = mm(PS[:, (0, 4, 1)[bt], c:c + 128], KBE[:, u, :], TTm[:, u, :], start=True, stop=True)
                r.then_inc(S("w_mm"), 1)
            for u in range(4):
                r = mm(PS[:, 2, 128 * u:128 * u + 128], TTm[:, u, :], BV[:, u, :], start=True, stop=True)
            r.then_inc(S("vn_mm"), 1)
            eng.wait_ge(S("nw"), 3)
            mm(PS[:, 3, 0:128], TTm[:, 8, :], BV[:, 8, :], start=True, stop=False, skip_group_check=True)
            for h in range(4):
                r = mm(PS[32 * h:32 * h + 32, 3, 0:128], NW[:, 8, 32 * h:32 * h + 32], S0[:, h, :], start=False,
                       stop=(h == 3), skip_group_check=True)
            r.then_inc(S("vn_mm"), 1)
            eng.wait_ge(S("vn"), 1)
            eng.wait_ge(S("qe"), 3)
            for u in range(4):
                r = mm(PS[:, 6, 128 * u:128 * u + 128], DT[:, u, :], VN[:, u, :], start=True, stop=True)
            r.then_inc(S("o_mm"), 1)
            for u in range(4):
                r = mm(PS[:, 4, 128 * u:128 * u + 128], KDEC[:, u, :], VN[:, u, :], start=True, stop=True)
            r.then_inc(S("s_mm"), 1)
            eng.wait_ge(S("vn"), 2)
            mm(PS[:, 7, 0:128], DT[:, 8, :], VN[:, 8, :], start=True, stop=False, skip_group_check=True)
            for h in range(4):
                r = mm(PS[32 * h:32 * h + 32, 7, 0:128], E[:, 8, 32 * h:32 * h + 32], S0[:, h, :], start=False,
                       stop=(h == 3), skip_group_check=True)
            r.then_inc(S("o_mm"), 1)
            mm(PS[:, 0, :], KDEC[:, 8, :], VNm.rearrange("p a b -> p (a b)"), start=True, stop=True)\
                .then_inc(S("s_mm"), 1)
            eng.wait_ge(S("s1"), 1)
            for h in range(4):
                o = PS[:, 5, 128 * h:128 * h + 128]
                mm(o, TTm[:, 4 + h, :], BV[:, 4 + h, :], start=True, stop=False)
                r = mm(o, NW[:, 4 + h, :], S1[:, h, :], start=False, stop=True)
            r.then_inc(S("vn_mm"), 1)
            eng.wait_ge(S("vn"), 3)
            for h in range(4):
                o = PS[:, 1, 128 * h:128 * h + 128]
                mm(o, E[:, 4 + h, :], S1[:, h, :], start=True, stop=False)
                r = mm(o, DT[:, 4 + h, :], VN[:, 4 + h, :], start=False, stop=True)
            r.then_inc(S("o_mm"), 1)
            for h in range(4):
                r = mm(PS[:, 4, 128 * h:128 * h + 128], KDEC[:, 4 + h, :], VN[:, 4 + h, :], start=True, stop=True)
            r.then_inc(S("s_mm"), 1)
            for bt, (u0, u1) in enumerate(BT):
                eng.wait_ge(S("on"), bt + 1)
                for u in range(u0, u1):
                    c = 128 * (u - u0)
                    r = t_.transpose(PS[:, (2, 3, 5)[bt], c:c + 128], ON[:, u, :], ident[:, :])
                r.then_inc(S("on_tr"), 1)

            def out_proj(ps, upto=lambda kind, j: None):
                for j in range(8):
                    upto("out", j)
                    bb = (B_OUT0, B_OUT1, B_OUT1 + 48)[ps] + j
                    landed(bb)
                    for t in ((0, 1, 2), (2, 0), (1,))[ps]:
                        for k in range(KT):
                            r = mm(PS[:, 2 * t + j // 4, 128 * (j % 4):128 * (j % 4) + 128],
                                   mixT[:, k, 128 * t:128 * t + 128], blkw(bb % WSLOTS, k),
                                   start=(k == 0), stop=(k == KT - 1))
                    r.then_inc(S("blk"), 1)

            eng.wait_ge(S("mix_d"), 1)
            eng.wait_ge(S("mix_lru"), 1)
            eng.wait_ge(S("sfin"), 2)
            out_proj(0)
            transposes(1)

            def step(m, i=None):
                sl = m % UVS
                eng.wait_ge(S("diag"), at(i, m + 1))
                for half in range(2):
                    o = D + 512 * half
                    r = mm(PS[:, 6 + half, :], DG[:, sl, :], UV[:, sl, o:o + 512], start=False, stop=False,
                           skip_group_check=True)
                r.then_inc(S(f"uv_free{sl}"), 1)

            def begin(q):
                if q:
                    eng.wait_ge(S("x_peer"), q)
                for half in range(2):
                    mm(PS[:, 6 + half, :], ZR[:, 0:128], ZR[:, :], start=True, stop=False, skip_group_check=True)

            def end(q):
                for half in range(2):
                    r = mm(PS[:, 6 + half, :], ZR[:, 0:128], ZR[:, :], start=False, stop=True, skip_group_check=True)
                r.then_inc(S("acc"), 1)
                if UNITS[q][1] == 2:
                    for half in range(2):
                        eng.wait_ge(S("ys"), 2 * (q // 3) + half + 1)
                        r = mm(PS[:, 6 + half, :], RP[:, :], YS[:, 512 * half:512 * half + 512],
                               start=True, stop=True)
                    r.then_inc(S("acc"), 1)

            run = Steps(eng, step, begin, end)

            def lagging(m):
                edge = any(m - PE_LAG < u[2] <= m for u in UNITS)
                return m if edge else m - PE_LAG

            def queries(ps, upto):
                b0 = (B_Q0, B_Q1, B_Q1 + 48)[ps]
                c0, nq = ((0, NT), (0, 160), (256, 128))[ps]

                def score(j):
                    eng.wait_ge(S("qt"), 16 * ps + j + 1)
                    if j >= 4:
                        eng.wait_ge(S("sc"), 16 * ps + j - 3)
                    q = 32 * ((j // 2) % 4)
                    kt = keysT[:, min(ps, 1), j % 2, :]
                    bk = PS[:, j % 4, :]
                    if ps < 2:
                        mm(bk[:, 0:128], QT[:, j % 4, 0:128], kt, start=True, stop=True)
                        o = (NP, 128)[ps]
                        r = mm(bk[q:q + 32, 256:384], QT[:, j % 4, o:o + 32], kt, start=True, stop=True)
                    if ps != 1:
                        o = (128, 0, 0)[ps]
                        r = mm(bk[:, 128:256], QT[:, j % 4, o:o + 128], kt, start=True, stop=True)
                    r.then_inc(S("sc_mm"), 1)
                for j in range(16):
                    upto("q", j)
                    if j >= 2:
                        eng.wait_ge(S("qt"), 16 * ps + j - 1)
                    block_fm(b0 + j, 4 + j % 2, c0, nq)
                    if j >= 1:
                        score(j - 1)
                score(15)

            queries(0, lambda kind, j: None)
            run.loop(0, 2)
            run.loop(32, 8)

            def mixer1(ps):
                def upto(kind, j=0):
                    run.upto(lagging(PLAN[ps, kind, j]))
                W_ = (128, 256)[ps]
                upto("norm2")
                transposes(2 + 2 * ps)
                c0, nq = ((0, 160), (256, 128))[ps]
                for j in range(24):
                    upto("qkv", j)
                    if j >= 4:
                        eng.wait_ge(S("ev1"), 24 * ps + j - 3)
                    bb = B_QKV + 48 * ps + j
                    if j < 16:
                        block_fm(bb, j % 4, c0, nq)
                    else:
                        landed(bb)
                        for i, c in enumerate(((0, 128), (256,))[ps]):
                            for k in range(KT):
                                r = mm(PS[:, j % 4, 128 * i:128 * i + 128], hT[:, k, c:c + 128],
                                       blkw(bb % WSLOTS, k), start=(k == 0), stop=(k == KT - 1))
                        r.then_inc(S("blk"), 1)
                eng.wait_ge(S("ev1"), 24 * ps + 24)

                def qk(h):
                    if h >= 2:
                        eng.wait_ge(S("sexp"), 16 * ps + 2 * (h - 1))
                    for c in range(2):
                        o = PS[:, h % 2, W_ * c:W_ * c + W_]
                        mm(o, QZ[:, 2 * h + c, 0:128], KTt[:, h, 0:W_], start=True, stop=False, skip_group_check=True)
                        r = mm(o[:, W_ - 128:W_], ident[:, :], msk, start=False, stop=True, skip_group_check=True)
                    r.then_inc(S("s_qk"), 1)

                def p_transposes(h):
                    eng.wait_ge(S("pc"), 8 * ps + h + 1)
                    for i in range(W_ // 128):
                        r = t_.transpose(PS[:, 4 + h % 2, 128 * i:128 * i + 128],
                                         PC[:, h % 2, 128 * i:128 * i + 128], ident[:, :])
                    r.then_inc(S("p_tr"), 1)

                def pv(h):
                    eng.wait_ge(S("pt"), 8 * ps + h + 1)
                    c = 128 * (h % 4)
                    for i in range(W_ // 128):
                        r = mm(PS[:, 2 + h // 4, c:c + 128], PTt[:, h % 2, 128 * i:128 * i + 128],
                               Vt[:, i, 128 * h:128 * h + 128], start=(i == 0), stop=(i == W_ // 128 - 1))
                    r.then_inc(S("pv"), 1)

                for h in range(HC + 2):
                    upto("head", h)
                    if h < HC:
                        qk(h)
                    if 1 <= h <= HC:
                        p_transposes(h - 1)
                    if h >= 2:
                        pv(h - 2)
                if ps == 0:
                    eng.wait_ge(S("sexp"), 2 * HC)
                    eng.wait_ge(S("os"), 2)
                for gq in range(2 * (1 - ps)):
                    upto("smp", 2 * gq)
                    eng.wait_ge(S("kc"), 16 * (gq + 1))
                    eng.wait_ge(S("vc"), 16 * (gq + 1))
                    if gq:
                        eng.wait_ge(S("ssexp"), 2)
                    for c in range(2):
                        for j in range(4):
                            h = 4 * gq + j
                            qz = QZ[:, 2 * h + c, 128:160]
                            mm(PS[32 * j:32 * j + 32, 2 * c, :], qz, KC[:, j, :], start=True, stop=True)
                            r = mm(PS[32 * j:32 * j + 32, 2 * c + 1, 0:32], qz, KTt[:, h, NP:NT], start=True, stop=True)
                    r.then_inc(S("s_qks"), 1)
                    upto("smp", 2 * gq + 1)
                    eng.wait_ge(S("pcs"), gq + 1)
                    if gq:
                        eng.wait_ge(S("os"), 3)
                    for i in range(4):
                        t_.transpose(PS[:, 4, 128 * i:128 * i + 128], PCs[:, 0, 128 * i:128 * i + 128], ident[:, :])
                    t_.transpose(PS[0:32, 5, 0:128], PCs[:, 0, 512:544], ident[:, :]).then_inc(S("ps_tr"), 1)
                    eng.wait_ge(S("pts"), gq + 1)
                    ptf = PTt.rearrange("p a b -> p (a b)")
                    for j in range(4):
                        o = PS[32 * j:32 * j + 32, 5, 128:256]
                        for i in range(4):
                            mm(o, ptf[:, 128 * i + 32 * j:128 * i + 32 * j + 32], VC[:, i, 128 * j:128 * j + 128],
                               start=(i == 0), stop=False)
                        h = 4 * gq + j
                        r = mm(o, ptf[0:32, 512 + 32 * j:512 + 32 * j + 32], Vt[0:32, 2, 128 * h:128 * h + 128],
                               start=False, stop=True)
                    r.then_inc(S("pvs"), 1)
                upto("on")
                eng.wait_ge(S("os_n"), ps + 1)
                for i in range((3, 2)[ps]):
                    for u in range((4, 4, 2)[i]):
                        src = Hn[:, ps, 512 * i + 128 * u:512 * i + 128 * u + 128] if i < 2 \
                            else Hn[:, 2, 128 * u:128 * u + 128]
                        r = t_.transpose(PS[:, (0, 1, 4)[i], 128 * u:128 * u + 128], src, ident[:, :])
                    r.then_inc(S("o_tr"), 1)
                eng.wait_ge(S("mix1"), (10, 12)[ps])
                out_proj(1 + ps, upto)
                upto("norm3")
                transposes(3 + 2 * ps)
                queries(1 + ps, upto)

            mixer1(0)
            run.upto(AHEAD)
            mixer1(1)
            run.upto(448)
            run.loop(448, 8)


def layout(inputs):
    import numpy as np
    f = {k: np.asarray(v) for k, v in inputs.items()}
    tile = lambda v, n: np.concatenate([v] * n, axis=0)
    pcol = lambda v: np.ascontiguousarray(v.reshape(-1, 128).T)
    xs = f["x_sample"][0]
    x = np.stack([f["x_prompt"][0, 0:128], f["x_prompt"][0, 128:256], tile(xs, 4)], axis=1)
    blk = lambda w: np.ascontiguousarray(w.reshape(8, 128, -1, 128).transpose(2, 1, 0, 3)).reshape(-1, 128, 1024)
    wi = f["ab_w_in"][0]
    w = np.concatenate([blk(wi[:, 0:2048]), blk(wi[:, 2056:3080]), blk(f["ab_w_out"][0]), blk(f["peer_w_query"][0]),
                        blk(f["c_w_qkv"][0]), blk(f["c_w_out"][0]), blk(f["peer_w_query"][1])])
    assert w.shape[0] == NBLK
    wba = np.ascontiguousarray(wi[:, 2048:2056].reshape(8, 128, 8).transpose(1, 0, 2)).reshape(128, 64)
    cw = np.concatenate([f["a_conv_w"][0], f["b_conv_w"][0]], axis=1)
    cw = cw.reshape(4, 16, 128).transpose(2, 1, 0).reshape(128, 64)
    heads = lambda v: np.concatenate([np.broadcast_to(v[None, :], (128, 4))] * 2 + [np.repeat(v, 32)[:, None]], axis=1)
    cols = np.concatenate([
        cw, pcol(f["b_conv_b"][0]), heads(f["a_log"][0]), heads(f["a_dt_bias"][0]), pcol(f["b_lambda"][0]),
        pcol(f["b_gate_a_b"][0]), pcol(f["b_gate_x_b"][0]), f["a_norm"][0][:, None], f["c_norm"][0][:, None],
        pcol(f["state_b_rglru"][0, 0])], axis=1)
    assert cols.shape == (128, NCOL)
    st = np.concatenate([f["state_a_conv"][0, 0], f["state_b_conv"][0, 0]], axis=1)
    st = st.reshape(3, 16, 128).transpose(2, 1, 0).reshape(128, 48)
    gw = np.zeros((128, 2, 4, 128), np.float32)
    for i, n in enumerate(("b_gate_a_w", "b_gate_x_w")):
        for q in range(8):
            o = 64 * (q % 2)
            gw[o:o + 64, i, q // 2, o:o + 64] = f[n][0, q]
    c = np.ascontiguousarray
    return {
        "x": c(x), "w": w, "wba": wba, "cols": c(cols), "st_conv": c(st), "gw": gw.reshape(128, 1024),
        "gains": np.stack([f["norm_mix"][0], f["norm_ffn"][0], f["norm_mix"][1], f["norm_ffn"][1], f["norm_final"]]),
        "s0": c(f["state_a_delta"][0, 0].transpose(1, 0, 2)).reshape(128, 512),
        "keys": c(f["peer_sub_keys"].transpose(3, 0, 1, 2)).reshape(128, 512),
        "uv0": np.concatenate([f["peer_u"][0], f["peer_v"][0]], axis=1),
        "uv1": np.concatenate([f["peer_u"][1], f["peer_v"][1]], axis=1),
        "lq": np.stack([f["c_lambda_q1"][0], f["c_lambda_q2"][0], f["c_lambda_k1"][0], f["c_lambda_k2"][0]])
        .reshape(1, 256),
        "kc": c(f["cache_c_k"][0, 0].reshape(512, 8, 128).transpose(2, 1, 0)).reshape(128, 4096),
        "vc": c(f["cache_c_v"][0, 0].reshape(4, 128, 1024).transpose(1, 0, 2)).reshape(128, 4096),
    }


OUTS = {"o_y": (128, 3, 1024), "o_conv": (128, 96), "o_dp": (128, 512), "o_ds": (128, 512), "o_h": (128, 8),
        "o_k": (128, 8 * 288), "o_v": (128, 3 * 1024)}


def kernel(**inputs):
    import numpy as np
    import concourse.bacc as bacc
    from concourse import mybir
    from concourse.bass_utils import run_bass_kernel_spmd as run

    nc = bacc.Bacc("TRN2", target_bir_lowering=False, num_devices=1)
    arrays = layout(inputs)
    outs = dict(OUTS)
    F = mybir.dt.float32
    T = {k: nc.dram_tensor("in_" + k, v.shape, F, kind="ExternalInput").ap() for k, v in arrays.items()}
    T.update({k: nc.dram_tensor("out_" + k, s, F, kind="ExternalOutput").ap() for k, s in outs.items()})
    build(nc, T)
    r = run(nc, [{"in_" + k: v for k, v in arrays.items()}], core_ids=[0]).results[0]
    r = {k: r["out_" + k] for k in outs}
    y = r["o_y"].reshape(128, 3, 1024)
    yp = np.concatenate([y[:, 0], y[:, 1]])[None]
    ys = y[0:32, 2][None]
    cs = r["o_conv"].reshape(128, 16, 2, 3).transpose(2, 3, 1, 0).reshape(2, 3, 2048)
    ds = [r[n].reshape(128, 4, 128).transpose(1, 0, 2)[None, None] for n in ("o_dp", "o_ds")]
    hs = r["o_h"].reshape(128, 4, 2).transpose(2, 1, 0).reshape(2, 512)
    k = r["o_k"].reshape(128, 8, 288).transpose(2, 1, 0)
    v = r["o_v"].reshape(128, 3, 1024)
    vp = np.concatenate([v[:, 0], v[:, 1]])
    return (yp, ys, cs[0, :, 0:1536][None, None], ds[0], cs[0, :, 1536:][None, None], hs[0][None, None],
            k[0:256].reshape(1, 1, 256, 8, 2, 64), vp.reshape(1, 1, 256, 8, 128),
            cs[1, :, 0:1536][None, None], ds[1], cs[1, :, 1536:][None, None], hs[1][None, None],
            k[256:].reshape(1, 1, 32, 8, 2, 64), v[0:32, 2].reshape(1, 1, 32, 8, 128))
```
